# Optimizing a Trainium2 kernel written in Bass

```python
import math
import jax, jax.numpy as jnp
from jax import lax
import numpy as np

D_MODEL = 1024
BATCH = 1
SEQ = 512
DEPTH = 1

HEAD_DIM = 64
FOX_HEADS = 4
DIFF_HEADS = 4
DIL_HEADS = 8
FOX_W = FOX_HEADS * HEAD_DIM
DIFF_W = DIFF_HEADS * HEAD_DIM
DIL_W = DIL_HEADS * HEAD_DIM
MIX_W = FOX_W + DIFF_W + DIL_W
DIFF_QK_DIM = HEAD_DIM // 2
IN_COLS = 3 * MIX_W + FOX_HEADS
Q_BLOCK = 128
DIL_CONFIGS = ((128, 1), (512, 4), (2048, 16))
MEM_TOKENS = 256
MEM_HEADS = 4
MEM_HEAD_DIM = D_MODEL // MEM_HEADS
D_FF = 2816
CONV_WIDTH = 3
ALPHA = (2 * DEPTH) ** 0.25
BETA = (8 * DEPTH) ** -0.25
LN_EPS = 1e-5
NEG_INF = -1e30
FORGET_BIAS_INIT = 3.0

kernel_name = 'hybrid_fox_diff_dilated_postnorm_decoder'

def layer_norm(x, g, b):
    xf = x.astype(jnp.float32)
    mu = jnp.mean(xf, axis=-1, keepdims=True)
    var = jnp.mean(jnp.square(xf - mu), axis=-1, keepdims=True)
    y = (xf - mu) * lax.rsqrt(var + LN_EPS) * g.astype(jnp.float32) + b.astype(jnp.float32)
    return y.astype(x.dtype)

def rms_norm(x, g):
    xf = x.astype(jnp.float32)
    return xf * lax.rsqrt(jnp.mean(jnp.square(xf), axis=-1, keepdims=True) + LN_EPS) * g.astype(jnp.float32)

def alibi_slopes():
    n = DIFF_HEADS + DIL_HEADS
    slopes = 2.0 ** (-8.0 * np.arange(1, n + 1) / n)
    stride = n // DIFF_HEADS
    diff_sel = np.arange(0, n, stride)[:DIFF_HEADS]
    dil_sel = np.setdiff1d(np.arange(n), diff_sel)
    return (jnp.asarray(slopes[diff_sel], dtype=jnp.float32),
            jnp.asarray(slopes[dil_sel], dtype=jnp.float32))

def fox_attention(q, k, v, f_logit, b_f):
    B, S, H, Dh = q.shape
    log_f = jax.nn.log_sigmoid(f_logit.astype(jnp.float32) + b_f.astype(jnp.float32))
    c = jnp.cumsum(log_f, axis=1).transpose(0, 2, 1)
    kpos = jnp.arange(S)
    scale = Dh ** -0.5

    def block(i):
        start = i * Q_BLOCK
        qb = lax.dynamic_slice_in_dim(q, start, Q_BLOCK, axis=1)
        cb = lax.dynamic_slice_in_dim(c, start, Q_BLOCK, axis=2)
        s = jnp.einsum('bqhd,bkhd->bhqk', qb, k).astype(jnp.float32) * scale
        qpos = start + jnp.arange(Q_BLOCK)
        causal = kpos[None, :] <= qpos[:, None]
        s = jnp.where(causal, s + cb[..., :, None] - c[..., None, :], NEG_INF)
        p = jax.nn.softmax(s, axis=-1)
        return jnp.einsum('bhqk,bkhd->bqhd', p.astype(v.dtype), v)

    out = lax.map(block, jnp.arange(S // Q_BLOCK))
    return out.transpose(1, 0, 2, 3, 4).reshape(B, S, H, Dh)

def diff_attention(q, k, v, slopes, lam, norm_g, lam_init):
    B, S, H, Dh = v.shape
    kpos = jnp.arange(S)
    scale = DIFF_QK_DIM ** -0.5

    def block(i):
        start = i * Q_BLOCK
        qb = lax.dynamic_slice_in_dim(q, start, Q_BLOCK, axis=1)
        s = jnp.einsum('bqhcd,bkhcd->bhcqk', qb, k).astype(jnp.float32) * scale
        qpos = start + jnp.arange(Q_BLOCK)
        dist = qpos[:, None] - kpos[None, :]
        alibi = -slopes[:, None, None, None] * dist
        s = jnp.where(dist >= 0, s + alibi, NEG_INF)
        p = jax.nn.softmax(s, axis=-1)
        w = p[:, :, 0] - lam * p[:, :, 1]
        return jnp.einsum('bhqk,bkhd->bqhd', w.astype(v.dtype), v)

    out = lax.map(block, jnp.arange(S // Q_BLOCK))
    out = out.transpose(1, 0, 2, 3, 4).reshape(B, S, H, Dh)
    return (rms_norm(out, norm_g) * (1.0 - lam_init)).astype(v.dtype)

def strided_window_attention(q, k, v, slopes, window, dil):
    B, S, H, Dh = q.shape
    n_back = window // dil
    L = -(-S // dil)
    L = -(-L // Q_BLOCK) * Q_BLOCK
    Sp = L * dil
    nb = L // Q_BLOCK

    def strided(a):
        a = jnp.pad(a, ((0, 0), (0, Sp - S), (0, 0), (0, 0)))
        return a.reshape(B, L, dil, H, Dh).transpose(0, 2, 1, 3, 4).reshape(B, dil, nb, Q_BLOCK, H, Dh)

    def with_prev(a):
        prev = jnp.pad(a, ((0, 0), (0, 0), (1, 0), (0, 0), (0, 0), (0, 0)))[:, :, :-1]
        return jnp.concatenate([prev, a], axis=3)

    qs = strided(q)
    kb = with_prev(strided(k))
    vb = with_prev(strided(v))
    s = jnp.einsum('brnqhd,brnkhd->brnhqk', qs, kb).astype(jnp.float32) * (Dh ** -0.5)
    qi = jnp.arange(Q_BLOCK)
    ki = jnp.arange(2 * Q_BLOCK) - Q_BLOCK
    delta = qi[:, None] - ki[None, :]
    key_pos = jnp.arange(nb)[:, None] * Q_BLOCK + ki[None, :]
    valid = ((delta >= 0) & (delta <= n_back))[None] & (key_pos >= 0)[:, None, :]
    alibi = -slopes[:, None, None] * (dil * delta)
    s = jnp.where(valid[:, None], s + alibi, NEG_INF)
    m = jnp.max(s, axis=-1, keepdims=True)
    e = jnp.exp(s - m)
    den = jnp.sum(e, axis=-1, keepdims=True)
    o = jnp.einsum('brnhqk,brnkhd->brnqhd', (e / den).astype(v.dtype), vb)
    lse = (m + jnp.log(den))[..., 0]
    o = o.reshape(B, dil, L, H, Dh).transpose(0, 2, 1, 3, 4).reshape(B, Sp, H, Dh)[:, :S]
    lse = lse.transpose(0, 1, 2, 4, 3).reshape(B, dil, L, H).transpose(0, 2, 1, 3).reshape(B, Sp, H)[:, :S]
    return o, lse

def dilated_mixture_attention(q, k, v, slopes):
    outs, lses = [], []
    for window, dil in DIL_CONFIGS:
        o, lse = strided_window_attention(q, k, v, slopes, window, dil)
        outs.append(o)
        lses.append(lse)
    wts = jax.nn.softmax(jnp.stack(lses, 0), axis=0)
    out = jnp.einsum('cbsh,cbshd->bshd', wts, jnp.stack(outs, 0).astype(jnp.float32))
    return out.astype(v.dtype)

def memory_cross_attention(x, mem, w_q, w_kv, w_o):
    B, S, _ = x.shape
    M = mem.shape[1]
    q = (x @ w_q).reshape(B, S, MEM_HEADS, MEM_HEAD_DIM)
    k, v = jnp.split(mem @ w_kv, 2, axis=-1)
    k = k.reshape(B, M, MEM_HEADS, MEM_HEAD_DIM)
    v = v.reshape(B, M, MEM_HEADS, MEM_HEAD_DIM)
    s = jnp.einsum('bqhd,bkhd->bhqk', q, k).astype(jnp.float32) * (MEM_HEAD_DIM ** -0.5)
    p = jax.nn.softmax(s, axis=-1)
    o = jnp.einsum('bhqk,bkhd->bqhd', p.astype(v.dtype), v).reshape(B, S, D_MODEL)
    return o @ w_o

def conv_glu_ffn(x, w_up, conv_w, conv_b, w_down):
    u = x @ w_up
    u = lax.conv_general_dilated(u, conv_w, window_strides=(1,), padding=((CONV_WIDTH - 1, 0),),
                                 dimension_numbers=('NWC', 'WIO', 'NWC'),
                                 feature_group_count=2 * D_FF) + conv_b
    g, val = jnp.split(u, 2, axis=-1)
    return (jax.nn.gelu(g) * val) @ w_down

def setup_inputs(seed: int = 0) -> dict:
    key = jax.random.key(seed)
    ks = jax.random.split(key, 24)
    f32 = jnp.float32
    nrm = lambda k, shape, scale: jax.random.normal(k, shape, f32) * scale
    gain = lambda k, shape: 1.0 + 0.02 * jax.random.normal(k, shape, f32)
    return {
        'x': jax.random.normal(ks[0], (BATCH, SEQ, D_MODEL), f32),
        'mem': jax.random.normal(ks[1], (BATCH, MEM_TOKENS, D_MODEL), f32),
        'w_in': nrm(ks[2], (DEPTH, D_MODEL, IN_COLS), D_MODEL ** -0.5),
        'b_f': FORGET_BIAS_INIT + nrm(ks[3], (DEPTH, FOX_HEADS), 0.1),
        'lambda_q1': nrm(ks[4], (DEPTH, DIFF_QK_DIM), 0.1),
        'lambda_k1': nrm(ks[5], (DEPTH, DIFF_QK_DIM), 0.1),
        'lambda_q2': nrm(ks[6], (DEPTH, DIFF_QK_DIM), 0.1),
        'lambda_k2': nrm(ks[7], (DEPTH, DIFF_QK_DIM), 0.1),
        'diff_norm_g': gain(ks[8], (DEPTH, HEAD_DIM)),
        'w_o': nrm(ks[9], (DEPTH, MIX_W, D_MODEL), MIX_W ** -0.5 * BETA),
        'ln1_g': gain(ks[10], (DEPTH, D_MODEL)),
        'ln1_b': nrm(ks[11], (DEPTH, D_MODEL), 0.02),
        'w_mq': nrm(ks[12], (DEPTH, D_MODEL, D_MODEL), D_MODEL ** -0.5),
        'w_mkv': nrm(ks[13], (DEPTH, D_MODEL, 2 * D_MODEL), D_MODEL ** -0.5),
        'w_mo': nrm(ks[14], (DEPTH, D_MODEL, D_MODEL), D_MODEL ** -0.5 * BETA),
        'ln2_g': gain(ks[15], (DEPTH, D_MODEL)),
        'ln2_b': nrm(ks[16], (DEPTH, D_MODEL), 0.02),
        'w_up': nrm(ks[17], (DEPTH, D_MODEL, 2 * D_FF), D_MODEL ** -0.5),
        'conv_w': nrm(ks[18], (DEPTH, CONV_WIDTH, 1, 2 * D_FF), CONV_WIDTH ** -0.5),
        'conv_b': nrm(ks[19], (DEPTH, 2 * D_FF), 0.02),
        'w_down': nrm(ks[20], (DEPTH, D_FF, D_MODEL), D_FF ** -0.5 * BETA),
        'ln3_g': gain(ks[21], (DEPTH, D_MODEL)),
        'ln3_b': nrm(ks[22], (DEPTH, D_MODEL), 0.02),
    }

def reference(x, mem, w_in, b_f, lambda_q1, lambda_k1, lambda_q2, lambda_k2, diff_norm_g, w_o,
              ln1_g, ln1_b, w_mq, w_mkv, w_mo, ln2_g, ln2_b, w_up, conv_w, conv_b, w_down,
              ln3_g, ln3_b):
    B, S, _ = x.shape
    diff_slopes, dil_slopes = alibi_slopes()
    widths = [FOX_W, FOX_W, FOX_W, FOX_HEADS, DIFF_W, DIFF_W, DIFF_W, DIL_W, DIL_W, DIL_W]
    split_points = [int(p) for p in np.cumsum(widths)[:-1]]
    for l in range(DEPTH):
        h = x @ w_in[l]
        fq, fk, fv, ff, dq, dk, dv, cq, ck, cv = jnp.split(h, split_points, axis=-1)
        heads = lambda a, n: a.reshape(B, S, n, HEAD_DIM)
        fox_out = fox_attention(heads(fq, FOX_HEADS), heads(fk, FOX_HEADS), heads(fv, FOX_HEADS), ff, b_f[l])
        lam_init = 0.8 - 0.6 * math.exp(-0.3 * l)
        lam = (jnp.exp(jnp.sum(lambda_q1[l].astype(jnp.float32) * lambda_k1[l].astype(jnp.float32)))
               - jnp.exp(jnp.sum(lambda_q2[l].astype(jnp.float32) * lambda_k2[l].astype(jnp.float32)))
               + lam_init)
        diff_out = diff_attention(dq.reshape(B, S, DIFF_HEADS, 2, DIFF_QK_DIM),
                                  dk.reshape(B, S, DIFF_HEADS, 2, DIFF_QK_DIM),
                                  heads(dv, DIFF_HEADS), diff_slopes, lam, diff_norm_g[l], lam_init)
        dil_out = dilated_mixture_attention(heads(cq, DIL_HEADS), heads(ck, DIL_HEADS), heads(cv, DIL_HEADS), dil_slopes)
        mix = jnp.concatenate([fox_out, diff_out, dil_out], axis=2).reshape(B, S, MIX_W) @ w_o[l]
        x = layer_norm(ALPHA * x + mix, ln1_g[l], ln1_b[l])
        x = layer_norm(ALPHA * x + memory_cross_attention(x, mem, w_mq[l], w_mkv[l], w_mo[l]), ln2_g[l], ln2_b[l])
        x = layer_norm(ALPHA * x + conv_glu_ffn(x, w_up[l], conv_w[l], conv_b[l], w_down[l]), ln3_g[l], ln3_b[l])
    return x


_drawn_inputs = setup_inputs


def setup_inputs(seed=0):
    import zlib

    import numpy as np

    out = dict(_drawn_inputs(seed))
    spreads = {}
    factors = {'b_f': 64.0,
     'lambda_q1': 5.396,
     'lambda_k1': 6.806,
     'lambda_q2': 8.0,
     'lambda_k2': 8.0,
     'diff_norm_g': 23.374,
     'ln1_g': 2.785,
     'ln1_b': 2.704,
     'ln2_g': 2.726,
     'ln2_b': 2.734,
     'conv_b': 6.616,
     'ln3_g': 7.534,
     'ln3_b': 7.754}
    for name, (base, spread) in spreads.items():
        noise = np.random.default_rng([zlib.crc32(name.encode()), seed]).standard_normal(out[name].shape)
        drawn = base * np.exp(spread * noise) if base else spread * noise
        out[name] = __import__('jax').numpy.asarray(drawn.astype(out[name].dtype))
    for name, factor in factors.items():
        out[name] = (out[name] * factor).astype(out[name].dtype)
    return out
```

```python
from contextlib import ExitStack

import numpy as np

import concourse.bass as bass
from concourse import mybir

F32 = mybir.dt.float32
F32R = mybir.dt.float32r
I32 = mybir.dt.int32
ALU = mybir.AluOpType
ACT = mybir.ActivationFunctionType
AX = mybir.AxisListType

P = 128
SEQ = 512
D = 1024
MEM = 256
HD = 64
FOX, DIFF, DIL = 4, 4, 8
FOX_W, DIFF_W, DIL_W = FOX * HD, DIFF * HD, DIL * HD
HEADS = FOX + DIFF + DIL
D_FF = 2816
MEM_HEADS = 4
TT = SEQ // P
KT = D // P
MT = MEM // P
FT = D_FF // P
UNIT = 2048
HALF = 512
ALPHA = 2.0 ** 0.25
LN_EPS = 1e-5
NEG = -1e30
BIG = 3e38
LAM_INIT = 0.2
N_SLOPES = DIFF + DIL
SLOPES = [float(np.float32(2.0 ** (-8.0 * j / N_SLOPES))) for j in range(1, N_SLOPES + 1)]
DIFF_SLOPES = SLOPES[::N_SLOPES // DIFF]
DIL_SLOPES = [s for j, s in enumerate(SLOPES) if j % (N_SLOPES // DIFF)]

PHASES = [("qk", "fm", 8, 2), ("v", "tm", 4, 4), ("mk", "tm", 4, 2), ("wo", "tm", 4, 4),
          ("mv", "tm", 4, 2), ("mq", "fm", 4, 2), ("mo", "tm", 4, 4), ("up", "fm", 2 * FT // 2, 2),
          ("down", "tm", 12, 4)]
UNIT0, CHUNK0, CHUNKS = {}, {}, {}
_u = _c = 0
for _name, _kind, _n, _ch in PHASES:
    UNIT0[_name], CHUNK0[_name], CHUNKS[_name] = _u, _c, _ch
    _u, _c = _u + _n, _c + _n * _ch
N_UNITS = _u
DOWN_KT = [2, 4, 4, 4, 4, 4]
DOWN_K0 = [0, 2, 6, 10, 14, 18]


def chunks_through(phase, n):
    return CHUNK0[phase] + CHUNKS[phase] * n


HEAD_ORDER = [FOX + h for h in range(DIFF)] + list(range(FOX)) + list(range(FOX + DIFF, HEADS))
STEPS = [(hp, i) for hp in range(HEADS) for i in range(TT)]
N_STEPS = len(STEPS)


def is_diff(hp):
    return hp < DIFF


def is_fox(hp):
    return DIFF <= hp < DIFF + FOX


def maps_of(s):
    return [2 * s, 2 * s + 1] if is_diff(STEPS[s][0]) else [DIFF * TT + s]


N_MAPS = maps_of(N_STEPS - 1)[-1] + 1


def bias_item(s):
    hp, i = STEPS[s]
    if is_diff(hp):
        return hp
    if is_fox(hp):
        return DIFF + (hp - DIFF) * TT + i
    return DIFF + FOX * TT + hp - DIFF - FOX


N_ITEMS = bias_item(N_STEPS - 1) + 1
LAST_MAP_OF_ITEM = [max(maps_of(s)[-1] for s in range(N_STEPS) if bias_item(s) == n) for n in range(N_ITEMS)]
PAIR_LAG = 11
TURN_OF_STEP, TURN_OF_PAIR = {}, {}
for _k in range(N_STEPS + 4):
    if _k < N_STEPS:
        TURN_OF_STEP[_k] = len(TURN_OF_STEP) + len(TURN_OF_PAIR)
    if _k >= PAIR_LAG and (_k - PAIR_LAG) % 8 == 0:
        TURN_OF_PAIR[(_k - PAIR_LAG) // 8] = len(TURN_OF_STEP) + len(TURN_OF_PAIR)
STEP_OF_TURN = {t: s for s, t in TURN_OF_STEP.items()}
PAIR_OF_TURN = {t: p for p, t in TURN_OF_PAIR.items()}
S_BANKS = [4, 5, 0, 1]
T_BANKS = [6, 7]
O_BANKS = [2, 3]


def qk_place(hp, j):
    head = HEAD_ORDER[hp]
    if is_diff(hp):
        h = head - FOX
        return 4 + h // 2, 6 + h // 2, (h % 2) * HD + j * HD // 2, HD // 2
    if is_fox(hp):
        return head // 2, 2 + head // 2, (head % 2) * HD, HD
    g = head - FOX - DIFF
    tile = 8 + 4 * (g // 4) + (g % 4) // 2
    return tile, tile + 2, (g % 2) * HD, HD


def build_layer(nc, x, mem, w_in, b_f, lq1, lk1, lq2, lk2, diff_g, w_o, ln1_g, ln1_b, w_mq, w_mkv,
                w_mo, ln2_g, ln2_b, w_up, conv_w, conv_b, w_down, ln3_g, ln3_b, out):
    ctx = ExitStack()
    attention_memory = ExitStack()
    memory_memory = ExitStack()

    def sb(name, shape, dt=F32, stack=ctx):
        return stack.enter_context(nc.sbuf_tensor(name, shape, dt))

    def sem(name):
        return ctx.enter_context(nc.semaphore(name))

    with ctx:
        x_tok = sb("x_tok", [P, TT, D])
        act_hi = sb("act_hi", [P, KT, SEQ], F32R)
        act_lo = sb("act_lo", [P, KT, SEQ], F32R)
        raw = sb("raw", [P, 2, UNIT])
        w_hi = sb("w_hi", [P, 2, UNIT], F32R)
        w_lo = sb("w_lo", [P, 2, UNIT], F32R)
        scratch = sb("scratch", [P, 4, HALF])
        side = sb("side", [P, 4, HALF])
        ident = sb("ident", [P, P])
        conv_cols = sb("conv_cols", [P, 4, 2 * FT])
        ln_cols = sb("ln_cols", [P, 4, KT])
        eps = sb("eps", [P, 1])
        stats = sb("stats", [P, TT, 2, 6])
        mean_var = sb("mean_var", [P, TT, 2])
        ln_var = sb("ln_var", [P, TT])
        rstd = sb("rstd", [P, TT])
        mem_hi = sb("mem_hi", [P, KT, MEM], F32R, memory_memory)
        mem_lo = sb("mem_lo", [P, KT, MEM], F32R, memory_memory)
        mem_kt = sb("mem_kt", [P, KT, MEM], F32, memory_memory)
        am = attention_memory
        qk_t = sb("qk_t", [P, 16, SEQ], F32, am)
        v_tok = sb("v_tok", [P, TT, D], F32, am)
        prob = sb("prob", [P, 4, SEQ], F32, am)
        prob_t = sb("prob_t", [P, 2, SEQ], F32, am)
        o_tok = sb("o_tok", [P, TT, 2 * HD], F32, am)
        dist = sb("dist", [P, SEQ], F32, am)
        causal = sb("causal", [P, SEQ], F32, am)
        dil_mask = sb("dil_mask", [P, SEQ], F32, am)
        lam_s = sb("lam_s", [P, 6], F32, am)
        diff_gain = sb("diff_gain", [P, HD], F32, am)
        neg_max = sb("neg_max", [P, N_MAPS], F32, am)
        den = sb("den", [P, 2, N_STEPS], F32, am)
        mix_s = sb("mix_s", [P, 2, DIFF * TT], F32, am)
        rms_s = sb("rms_s", [P, 3, DIFF, TT], F32, am)
        forget_q = sb("forget_q", [P, TT, FOX], F32, am)
        wff = sb("wff", [P, KT, FOX], F32, am)
        wff_hi = sb("wff_hi", [P, KT, FOX], F32R, am)
        wff_lo = sb("wff_lo", [P, KT, FOX], F32R, am)
        bf_col = sb("bf_col", [FOX, 1], F32, am)
        am.close()
        cross = ExitStack()
        mem_v = sb("mem_v", [P, MT, D], F32, cross)
        xq_t = sb("xq_t", [P, KT, SEQ], F32, cross)
        xp = sb("xp", [P, 4, MEM], F32, cross)
        xp_t = sb("xp_t", [P, 2, MT, SEQ], F32, cross)
        x_neg_max = sb("x_neg_max", [P, MEM_HEADS * TT], F32, cross)
        x_den = sb("x_den", [P, MEM_HEADS * TT], F32, cross)
        x_rden = sb("x_rden", [P, MEM_HEADS * TT], F32, cross)
        cross.close()
        memory_memory.close()
        gate_hi = sb("gate_hi", [P, FT, SEQ], F32R)
        gate_lo = sb("gate_lo", [P, FT, SEQ], F32R)

        ps = ctx.enter_context(nc.psum_tensor("ps", [P, 8, HALF], F32))

        mem_tok = scratch[:, :, :].rearrange("p a b -> p (a b)").rearrange("p (m d) -> p m d", m=MT)
        side_rows = side[:, :, :].rearrange("p a b -> p (a b)").rearrange("p (r f) -> p r f", f=P)
        lam_in = side_rows[:, 8, :].rearrange("p (r d) -> p r d", r=4)
        side_gain = side[:, :, :].rearrange("p a b -> p (a b)").rearrange("p (m d) -> p m d", m=2)
        fg = prob[0:FOX, :, :]
        fsel = o_tok[0:FOX, :, :]

        x_loaded = [sem(f"x_loaded{t}") for t in range(TT)]
        mem_loaded = [sem(f"mem_loaded{t}") for t in range(MT)]
        gate_w_loaded = sem("gate_w_loaded")
        rows_loaded = sem("rows_loaded")
        lam_loaded = sem("lam_loaded")
        raw_loaded = [sem(f"raw_loaded{s}") for s in range(2)]
        gains_loaded = [sem(f"gains_loaded{n}") for n in range(3)]
        stored = sem("stored")
        ident_made = sem("ident_made")
        masks_zeroed = sem("masks_zeroed")
        masks_made = sem("masks_made")
        hi_split = sem("hi_split")
        split_done = sem("split_done")
        bias_scaled = sem("bias_scaled")
        bias_made = sem("bias_made")
        dense_done = sem("dense_done")
        x_turned = sem("x_turned")
        x_hi_done = sem("x_hi_done")
        x_lo_done = sem("x_lo_done")
        ff_summed = sem("ff_summed")
        gate_chain = sem("gate_chain")
        gate_exp = sem("gate_exp")
        forget_turned = sem("forget_turned")
        forget_q_ready = sem("forget_q_ready")
        forget_spread = sem("forget_spread")
        forget_k_ready = sem("forget_k_ready")
        rows_turned = sem("rows_turned")
        cols_ready = sem("cols_ready")
        lam_exp = sem("lam_exp")
        qk_evac = sem("qk_evac")
        v_evac = sem("v_evac")
        mk_evac = sem("mk_evac")
        mv_evac = sem("mv_evac")
        mq_evac = sem("mq_evac")
        mem_turned = sem("mem_turned")
        mem_hi_done = sem("mem_hi_done")
        mem_lo_done = sem("mem_lo_done")
        mk_turned = sem("mk_turned")
        mk_ready = sem("mk_ready")
        qk_done = sem("qk_done")
        scored = sem("scored")
        exp_done = sem("exp_done")
        mixed = sem("mixed")
        turned = sem("turned")
        prob_t_ready = sem("prob_t_ready")
        pv_done = sem("pv_done")
        o_normed = sem("o_normed")
        rms_summed = sem("rms_summed")
        rms_scaled = sem("rms_scaled")
        o_rmsed = sem("o_rmsed")
        o_hi_done = sem("o_hi_done")
        o_lo_done = sem("o_lo_done")
        res_done = [sem(f"res_done{n}") for n in range(3)]
        var_ready = [sem(f"var_ready{n}") for n in range(3)]
        rstd_ready = [sem(f"rstd_ready{n}") for n in range(3)]
        z_ready = [sem(f"z_ready{n}") for n in range(2)]
        z_turned = [sem(f"z_turned{n}") for n in range(2)]
        y_by_act = [sem(f"y_by_act{n}") for n in range(2)]
        y_by_vec = [sem(f"y_by_vec{n}") for n in range(2)]
        z_hi_done = [sem(f"z_hi_done{n}") for n in range(2)]
        z_lo_done = [sem(f"z_lo_done{n}") for n in range(2)]
        ln_applied = [sem(f"ln_applied{n}") for n in range(3)]
        xs_done = sem("xs_done")
        x_maxed = sem("x_maxed")
        x_exp_done = sem("x_exp_done")
        x_scaled = sem("x_scaled")
        xp_turned = sem("xp_turned")
        xp_t_ready = sem("xp_t_ready")
        xo_done = sem("xo_done")
        xo_hi_done = sem("xo_hi_done")
        xo_lo_done = sem("xo_lo_done")
        tap2_done = sem("tap2_done")
        tap1_done = sem("tap1_done")
        conv_done = sem("conv_done")
        gelu_done = sem("gelu_done")
        gated = sem("gated")
        gate_hi_done = sem("gate_hi_done")
        gate_lo_done = sem("gate_lo_done")
        mask_step = sem("mask_step")
        count_ready = sem("count_ready")
        count_ln = sem("count_ln")
        dil_mask_made = sem("dil_mask_made")
        lam_summed = sem("lam_summed")
        eps_set = sem("eps_set")
        vec_step = sem("vec_step")
        act_step = sem("act_step")

        def fm_src(w, c0, n):
            return w[0].rearrange("(k p) c -> p k c", p=P)[:, :, bass.ds(c0, n)]

        def tm_src(w, k0, nk, c0, n):
            return w[0].rearrange("(k p) c -> p k c", p=P)[:, k0:k0 + nk, bass.ds(c0, n)]

        def fm_slot(t, s):
            return t[:, s, :].rearrange("p (k c) -> p k c", k=KT)

        def tm_slot(t, s, nk=4):
            return t[:, s, 0:nk * HALF].rearrange("p (k c) -> p k c", k=nk)

        doubled = [UNIT0["v"], UNIT0["v"] + 1]

        def loaded_value(u):
            return 16 * (u // 2 + 1 + sum(1 for d in doubled if d % 2 == u % 2 and d <= u))

        FQ, FK, FV, FF = 0, FOX_W, 2 * FOX_W, 3 * FOX_W
        DQ = FF + FOX
        DK, DV = DQ + DIFF_W, DQ + 2 * DIFF_W
        CQ = DQ + 3 * DIFF_W
        CK, CV = CQ + DIL_W, CQ + 2 * DIL_W

        block = ctx.enter_context(nc.Block())

        @block.sync
        def _(sp):
            def load(u, dst, src, last_wait=None):
                if u >= 2:
                    sp.wait_ge(split_done, u - 1)
                sp.dma_start(dst, src).then_inc(raw_loaded[u % 2], 16)

            def load_tm_halves(phase, w, c0):
                for h in range(2):
                    for k in range(2):
                        load(UNIT0[phase] + 2 * h + k, tm_slot(raw, k), tm_src(w, 4 * k, 4, c0 + HALF * h, HALF))

            sp.dma_start(x_tok[:, 0, :], x[0, 0:P, :]).then_inc(x_loaded[0], 16)
            for t in range(1, TT):
                sp.dma_start(x_tok[:, t, :], x[0, t * P:(t + 1) * P, :]).then_inc(x_loaded[t], 16)
            for n, c in enumerate([FQ, FK, DQ, DK, CQ, CK, CQ + 256, CK + 256]):
                load(n, fm_slot(raw, n % 2), fm_src(w_in, c, 256))
            for k in range(2):
                load(UNIT0["v"] + k, tm_slot(raw, k)[:, :, 0:FOX_W], tm_src(w_in, 4 * k, 4, FV, FOX_W))
                sp.dma_start(tm_slot(raw, k)[:, :, FOX_W:HALF],
                             tm_src(w_in, 4 * k, 4, DV, DIFF_W)).then_inc(raw_loaded[k], 16)
            for k in range(2):
                load(UNIT0["v"] + 2 + k, tm_slot(raw, k), tm_src(w_in, 4 * k, 4, CV, HALF))
            load_tm_halves("mk", w_mkv, 0)
            load_tm_halves("wo", w_o, 0)
            sp.wait_ge(scored, N_MAPS)
            sp.dma_start(side_gain[:, 0, :], ln1_g.to_broadcast([P, D])).then_inc(gains_loaded[0], 16)
            sp.dma_start(side_gain[:, 1, :], ln1_b.to_broadcast([P, D])).then_inc(gains_loaded[0], 16)
            load_tm_halves("mv", w_mkv, D)
            for n in range(4):
                load(UNIT0["mq"] + n, fm_slot(raw, n % 2), fm_src(w_mq, 256 * n, 256))
            sp.wait_ge(ln_applied[0], TT)
            sp.dma_start(side_gain[:, 0, :], ln2_g.to_broadcast([P, D])).then_inc(gains_loaded[1], 16)
            sp.dma_start(side_gain[:, 1, :], ln2_b.to_broadcast([P, D])).then_inc(gains_loaded[1], 16)
            load_tm_halves("mo", w_mo, 0)
            u0 = UNIT0["up"]
            with sp.Fori(0, FT // 2) as t:
                for s in range(2):
                    sp.wait_ge(split_done, 2 * t + (u0 + s - 1))
                    sp.dma_start(fm_slot(raw, s), fm_src(w_up, 256 * t + s * D_FF, 256)).then_inc(raw_loaded[s], 16)
            u0 = UNIT0["down"]
            with sp.Fori(0, 2) as h:
                for n in range(6):
                    sp.wait_ge(split_done, 6 * h + (u0 + n - 1))
                    sp.dma_start(tm_slot(raw, n % 2, DOWN_KT[n]),
                                 tm_src(w_down, DOWN_K0[n], DOWN_KT[n], HALF * h, HALF)).then_inc(raw_loaded[n % 2], 16)
            sp.wait_ge(gate_lo_done, 2 + FT)
            sp.dma_start(side_gain[:, 0, :], ln3_g.to_broadcast([P, D])).then_inc(gains_loaded[2], 16)
            sp.dma_start(side_gain[:, 1, :], ln3_b.to_broadcast([P, D])).then_inc(gains_loaded[2], 16)
            for t in range(TT):
                sp.wait_ge(ln_applied[2], t + 1)
                sp.dma_start(out[0, t * P:(t + 1) * P, :], x_tok[:, t, :]).then_inc(stored, 16)
            sp.wait_ge(stored, 16 * TT)

        @block.gpsimd
        def _(pool):
            pool.memset(ident[:, :], 0.0).then_inc(masks_zeroed, 1)
            pool.memset(causal[:, :], 0.0).then_inc(masks_zeroed, 1)
            pool.memset(fsel.rearrange("p a b -> p (a b)"), 0.0).then_inc(masks_zeroed, 1)
            pool.wait_ge(masks_zeroed, 3)
            pool.affine_select(out=ident[:, :], in_=ident[:, :], compare_op=ALU.not_equal, fill=1.0, base=0,
                               pattern=[[-1, P]], channel_multiplier=1).then_inc(ident_made, 1)
            pool.iota(dist[:, :], [[-1, SEQ]], base=SEQ - P, channel_multiplier=1,
                      allow_small_or_imprecise_dtypes=True).then_inc(masks_made, 1)
            pool.affine_select(out=causal[:, :], in_=causal[:, :], compare_op=ALU.is_ge, fill=NEG, base=SEQ - P,
                               pattern=[[-1, SEQ]], channel_multiplier=1).then_inc(masks_made, 1)
            pool.affine_select(out=fsel, in_=fsel, compare_op=ALU.not_equal, fill=1.0, base=0,
                               pattern=[[-1, FOX], [0, P]], channel_multiplier=1).then_inc(masks_made, 1)
            pool.iota(prob[:, 3, :].bitcast(I32), [[-1, SEQ]], base=SEQ - P,
                      channel_multiplier=1).then_inc(masks_made, 1)

            def split(u, s, free_chunks, n=UNIT):
                pool.wait_ge(raw_loaded[s], loaded_value(u))
                if free_chunks is not None:
                    pool.wait_ge(dense_done, free_chunks)
                pool.tensor_scalar(w_hi[:, s, 0:n], raw[:, s, 0:n], 1.0, 0.0, ALU.mult, ALU.add).then_inc(hi_split, 1)
                pool.wait_ge(hi_split, u + 1)
                pool.tensor_tensor(w_lo[:, s, 0:n], raw[:, s, 0:n], w_hi[:, s, 0:n].bitcast(F32),
                                   ALU.subtract).then_inc(split_done, 1)

            chunks_to = [0] * (N_UNITS + 1)
            for name, _, n, ch in PHASES:
                for j in range(n):
                    chunks_to[UNIT0[name] + j + 1] = chunks_to[UNIT0[name] + j] + ch

            def split_units(first, last):
                for u in range(first, last):
                    split(u, u % 2, chunks_to[u - 1] if u >= 2 else None)

            split_units(0, UNIT0["wo"])

            def make_bias(n):
                slot = side[:, n % 4, :]
                if n == 0:
                    pool.wait_ge(cols_ready, 2)
                    pool.wait_ge(lam_exp, 1)
                if n >= 4:
                    pool.wait_ge(scored, LAST_MAP_OF_ITEM[n - 4] + 1)
                if DIFF <= n < DIFF + FOX * TT:
                    h, i = (n - DIFF) // TT, (n - DIFF) % TT
                    w = (i + 1) * P
                    if n == DIFF:
                        pool.wait_ge(forget_q_ready, 1)
                        pool.wait_ge(forget_k_ready, FOX)
                    pool.tensor_scalar(slot[:, 0:w], causal[:, SEQ - w:SEQ], forget_q[:, i, h:h + 1], 1.0,
                                       ALU.add, ALU.mult).then_inc(bias_scaled, 1)
                    pool.wait_ge(bias_scaled, n + 1)
                    pool.tensor_tensor(slot[:, 0:w], slot[:, 0:w], scratch[:, h, 0:w],
                                       ALU.subtract).then_inc(bias_made, 1)
                    return
                if n < DIFF:
                    slope, mask = DIFF_SLOPES[n], causal
                    pool.wait_ge(masks_made, 4)
                else:
                    slope, mask = DIL_SLOPES[n - DIFF - FOX * TT], dil_mask
                    pool.wait_ge(dil_mask_made, 1)
                pool.tensor_scalar(slot, dist[:, :], -slope, 1.0, ALU.mult, ALU.mult).then_inc(bias_scaled, 1)
                pool.wait_ge(bias_scaled, n + 1)
                pool.tensor_tensor(slot, slot, mask[:, :], ALU.add).then_inc(bias_made, 1)

            for n in range(N_ITEMS):
                make_bias(n)
                if n == DIFF + FOX * TT:
                    split_units(UNIT0["wo"], UNIT0["wo"] + 2)
            split_units(UNIT0["wo"] + 2, UNIT0["up"])
            rounded = pool.alloc_register("rounded")
            u0 = UNIT0["up"]
            pool.reg_mov(rounded, u0)
            with pool.Fori(0, FT // 2) as t:
                for s in range(2):
                    u = u0 + s
                    pool.wait_ge(raw_loaded[s], 16 * t + loaded_value(u))
                    pool.wait_ge(dense_done, 4 * t + (chunks_to[u0] + 2 * (s - 1)))
                    pool.reg_add(rounded, rounded, 1)
                    pool.tensor_scalar(w_hi[:, s, :], raw[:, s, :], 1.0, 0.0, ALU.mult, ALU.add).then_inc(hi_split, 1)
                    pool.wait_ge(hi_split, rounded)
                    pool.tensor_tensor(w_lo[:, s, :], raw[:, s, :], w_hi[:, s, :].bitcast(F32),
                                       ALU.subtract).then_inc(split_done, 1)
            u0 = UNIT0["down"]
            with pool.Fori(0, 2) as h:
                for n in range(6):
                    u, s, w = u0 + n, n % 2, DOWN_KT[n] * HALF
                    pool.wait_ge(raw_loaded[s], 48 * h + loaded_value(u))
                    pool.wait_ge(dense_done, chunks_to[u - 1])
                    pool.wait_ge(dense_done, 24 * h + (chunks_to[u0] + 4 * (n - 1)))
                    pool.reg_add(rounded, rounded, 1)
                    pool.tensor_scalar(w_hi[:, s, 0:w], raw[:, s, 0:w], 1.0, 0.0, ALU.mult,
                                       ALU.add).then_inc(hi_split, 1)
                    pool.wait_ge(hi_split, rounded)
                    pool.tensor_tensor(w_lo[:, s, 0:w], raw[:, s, 0:w], w_hi[:, s, 0:w].bitcast(F32),
                                       ALU.subtract).then_inc(split_done, 1)

        @block.tensor
        def _(pe):
            PASSES = [(w_hi, act_hi), (w_hi, act_lo), (w_lo, act_hi)]

            def fm_unit(s, done_value, bank, bank_free, act_parts=(act_hi, act_lo), width=SEQ):
                a_hi, a_lo = act_parts
                pe.wait_ge(split_done, done_value)
                for q in range(2):
                    bank_free(q)
                    for k in range(KT):
                        for n, (w, a) in enumerate([(w_hi, a_hi), (w_hi, a_lo), (w_lo, a_hi)]):
                            mm = pe.matmul(ps[:, bank + q, 0:width], fm_slot(w, s)[:, k, q * P:(q + 1) * P],
                                           a[:, k, 0:width], start=(k == 0 and n == 0),
                                           stop=(k == KT - 1 and n == 2))
                    mm.then_inc(dense_done, 1)

            def tm_unit(s, done_value, a_hi, a_lo, k0, nk, first, last, bank_free, tiles):
                pe.wait_ge(split_done, done_value)
                for t in range(tiles):
                    if first:
                        bank_free(t)
                    for k in range(nk):
                        for n, (w, a) in enumerate([(w_hi, a_hi), (w_hi, a_lo), (w_lo, a_hi)]):
                            mm = pe.matmul(ps[:, t, :], a[:, k0 + k, t * P:(t + 1) * P], tm_slot(w, s, nk)[:, k, :],
                                           start=(first and k == 0 and n == 0),
                                           stop=(last and k == nk - 1 and n == 2))
                    mm.then_inc(dense_done, 1)

            def tm_phase(phase, evac, a_hi=act_hi, a_lo=act_lo, tiles=TT):
                pe.sem_inc(evac, tiles)
                with pe.Fori(0, 2) as h:
                    for k in range(2):
                        tm_unit(k, 2 * h + (UNIT0[phase] + k + 1), a_hi, a_lo, 4 * k, 4, k == 0, k == 1,
                                lambda t: pe.wait_ge(evac, tiles * h + (t + 1)), tiles)

            def fm_phase(phase, evac, pairs):
                pe.sem_inc(evac, 4)
                with pe.Fori(0, pairs) as t:
                    for s in range(2):
                        fm_unit(s, 2 * t + (UNIT0[phase] + s + 1), 2 * s,
                                lambda q, s=s: pe.wait_ge(evac, 4 * t + (2 * s + q + 1)))

            pe.wait_ge(ident_made, 1)
            for n in range(2 * TT):
                t, g = n // 2, n % 2
                if g == 0:
                    pe.wait_ge(x_loaded[t], 16)
                if n >= 4:
                    pe.wait_ge(x_lo_done, n - 3)
                for k in range(4):
                    mm = pe.transpose(ps[:, 4 + n % 4, k * P:(k + 1) * P],
                                      x_tok[:, t, (4 * g + k) * P:(4 * g + k + 1) * P], ident[:, :])
                mm.then_inc(x_turned, 1)
            pe.wait_ge(x_lo_done, 2 * TT)
            pe.wait_ge(gate_chain, 2)
            for k in range(KT):
                for n, (w, a) in enumerate([(wff_hi, act_hi), (wff_hi, act_lo), (wff_lo, act_hi)]):
                    mm = pe.matmul(ps[0:FOX, 4, :], w[:, k, :], a[:, k, :], start=(k == 0 and n == 0),
                                   stop=(k == KT - 1 and n == 2))
            mm.then_inc(ff_summed, 1)
            fm_phase("qk", qk_evac, 4)
            pe.wait_ge(gate_chain, 6)
            for i in range(TT):
                mm = pe.transpose(ps[:, 5, i * FOX:(i + 1) * FOX], fg[:, 2, i * P:(i + 1) * P],
                                  ident[0:FOX, 0:FOX])
            mm.then_inc(forget_turned, 1)
            pe.wait_ge(rows_loaded, 16 * 8)
            for r in range(8):
                n = 2 * FT if r < 4 else KT
                mm = pe.transpose(ps[:, 6, r * 2 * FT:r * 2 * FT + n], side_rows[0:n, r, :], ident[0:n, 0:n])
            mm.then_inc(rows_turned, 1)
            pe.wait_ge(qk_evac, 4 + 16)
            tm_phase("v", v_evac)
            for n in range(2 * MT):
                t, g = n // 2, n % 2
                if g == 0:
                    pe.wait_ge(mem_loaded[t], 16)
                if n < 2:
                    pe.wait_ge(forget_q_ready, 1)
                    pe.wait_ge(cols_ready, 2)
                for k in range(4):
                    mm = pe.transpose(ps[:, 4 + n, k * P:(k + 1) * P],
                                      mem_tok[:, t, (4 * g + k) * P:(4 * g + k + 1) * P], ident[:, :])
                mm.then_inc(mem_turned, 1)
            pe.wait_ge(v_evac, 4 + 8)
            pe.wait_ge(mem_lo_done, 2 * MT)
            tm_phase("mk", mk_evac, mem_hi, mem_lo, MT)
            pe.wait_ge(mk_evac, MT + 4)
            for n in range(4):
                for f in range(2):
                    for m in range(MT):
                        c = (2 * n + f) * P
                        mm = pe.transpose(ps[:, 4 + n, (2 * f + m) * P:(2 * f + m + 1) * P],
                                          mem_tok[:, m, c:c + P], ident[:, :])
                mm.then_inc(mk_turned, 1)
            pe.wait_ge(masks_made, 3)
            for h in range(FOX):
                pe.wait_ge(mk_ready, h + 1)
                pe.matmul(ps[:, 4 + h, :], fsel[:, h, :], fg[:, 2, :], start=True, stop=True).then_inc(forget_spread, 1)

            def scores(s):
                hp, i = STEPS[s]
                for j, m in enumerate(maps_of(s)):
                    if m < 2:
                        pe.wait_ge(forget_k_ready, FOX)
                    if m >= 4:
                        pe.wait_ge(scored, m - 3)
                    tq, tk, r, d = qk_place(hp, j)
                    pe.matmul(ps[:, S_BANKS[m % 4], 0:(i + 1) * P], qk_t[r:r + d, tq, i * P:(i + 1) * P],
                              qk_t[r:r + d, tk, 0:(i + 1) * P], start=True, stop=True).then_inc(qk_done, 1)

            def turn_bank_free(turn):
                last = turn - 2
                if last in STEP_OF_TURN:
                    pe.wait_ge(prob_t_ready, STEP_OF_TURN[last] + 1)
                elif last in PAIR_OF_TURN:
                    pe.wait_ge(o_lo_done, PAIR_OF_TURN[last] + 1)

            def turn_probs(s):
                hp, i = STEPS[s]
                turn = TURN_OF_STEP[s]
                turn_bank_free(turn)
                if is_diff(hp):
                    pe.wait_ge(mixed, s + 1)
                else:
                    pe.wait_ge(exp_done, maps_of(s)[0] + 1)
                for b in range(i + 1):
                    mm = pe.transpose(ps[:, T_BANKS[turn % 2], b * P:(b + 1) * P],
                                      prob[:, maps_of(s)[0] % 4, b * P:(b + 1) * P], ident[:, :])
                mm.then_inc(turned, 1)

            def weigh_values(s):
                hp, i = STEPS[s]
                head = HEAD_ORDER[hp]
                pe.wait_ge(prob_t_ready, s + 1)
                if i == 0 and hp >= 2:
                    if is_diff(hp - 2):
                        pe.wait_ge(rms_summed, hp - 1)
                    else:
                        pe.wait_ge(o_normed, hp - 1)
                for b in range(i + 1):
                    mm = pe.matmul(ps[:, O_BANKS[hp % 2], i * HD:(i + 1) * HD], prob_t[:, s % 2, b * P:(b + 1) * P],
                                   v_tok[:, b, head * HD:(head + 1) * HD], start=(b == 0), stop=(b == i))
                mm.then_inc(pv_done, 1)

            def turn_pair(p):
                turn = TURN_OF_PAIR[p]
                turn_bank_free(turn)
                if is_diff(2 * p):
                    pe.wait_ge(o_rmsed, 2 * p + 2)
                else:
                    pe.wait_ge(o_normed, 2 * p + 2)
                for i in range(TT):
                    mm = pe.transpose(ps[:, T_BANKS[turn % 2], i * P:(i + 1) * P], o_tok[:, i, :], ident[:, :])
                mm.then_inc(turned, 1)

            scores(0)
            scores(1)
            for k in range(N_STEPS + 4):
                if k + 2 < N_STEPS:
                    scores(k + 2)
                if k < N_STEPS:
                    turn_probs(k)
                if 1 <= k <= N_STEPS:
                    weigh_values(k - 1)
                if k >= PAIR_LAG and (k - PAIR_LAG) % 8 == 0:
                    turn_pair((k - PAIR_LAG) // 8)

            def turn_z(n):
                pe.wait_ge(z_ready[n], TT)
                for k in range(KT):
                    if k >= 4:
                        pe.wait_ge([y_by_act, y_by_vec][k % 2][n], k // 2 - 1)
                    for t in range(TT):
                        mm = pe.transpose(ps[:, 4 + k % 4, t * P:(t + 1) * P], x_tok[:, t, k * P:(k + 1) * P],
                                          ident[:, :])
                    mm.then_inc(z_turned[n], 1)

            pe.wait_ge(o_lo_done, HEADS // 2)
            tm_phase("wo", res_done[0])
            pe.wait_ge(res_done[0], 4 + 8)
            tm_phase("mv", mv_evac, mem_hi, mem_lo, MT)
            turn_z(0)
            pe.wait_ge(z_lo_done[0], KT)
            pe.wait_ge(mv_evac, MT + 4)
            fm_phase("mq", mq_evac, 2)

            def x_scores(c):
                h, i = c // TT, c % TT
                if c == 0:
                    pe.wait_ge(mq_evac, 4 + KT)
                if c >= 2:
                    pe.wait_ge(x_exp_done, c - 1)
                for f in range(2):
                    mm = pe.matmul(ps[:, 4 + c % 2, 0:MEM], xq_t[:, 2 * h + f, i * P:(i + 1) * P],
                                   mem_kt[:, 2 * h + f, :], start=(f == 0), stop=(f == 1))
                mm.then_inc(xs_done, 1)

            def x_turn(c):
                if c % 2 == 0 and c >= 4:
                    pe.wait_ge(xp_t_ready, c // 2 - 1)
                pe.wait_ge(x_scaled, c + 1)
                for m in range(MT):
                    mm = pe.transpose(ps[:, 6 + (c // 2) % 2, ((c % 2) * MT + m) * P:((c % 2) * MT + m + 1) * P],
                                      xp[:, c % 4, m * P:(m + 1) * P], ident[:, :])
                mm.then_inc(xp_turned, 1)

            def x_weigh(h):
                pe.wait_ge(xp_t_ready, 2 * h + 2)
                for f in range(2):
                    if h >= 2:
                        pe.wait_ge(xo_lo_done, 2 * (h - 2) + f + 1)
                    for m in range(MT):
                        c = (2 * h + f) * P
                        mm = pe.matmul(ps[:, 2 * (h % 2) + f, :], mem_v[:, m, c:c + P], xp_t[:, h % 2, m, :],
                                       start=(m == 0), stop=(m == MT - 1))
                    mm.then_inc(xo_done, 1)

            N_X = MEM_HEADS * TT
            x_scores(0)
            x_scores(1)
            for c in range(N_X + 2):
                if c + 2 < N_X:
                    x_scores(c + 2)
                if c < N_X:
                    x_turn(c)
                if c >= TT + 1 and (c - TT - 1) % TT == 0:
                    x_weigh((c - TT - 1) // TT)
            pe.wait_ge(xo_lo_done, KT)
            tm_phase("mo", res_done[1])
            turn_z(1)
            pe.wait_ge(z_lo_done[1], KT)
            pe.wait_ge(res_done[1], 4 + 8)

            fm_phase("up", conv_done, FT // 2)
            pe.wait_ge(conv_done, 4 + 2 * FT)
            pe.wait_ge(gate_lo_done, 2 + FT)
            pe.sem_inc(res_done[2], 4)
            with pe.Fori(0, 2) as h:
                for n in range(6):
                    tm_unit(n % 2, 6 * h + (UNIT0["down"] + n + 1), gate_hi, gate_lo, DOWN_K0[n], DOWN_KT[n],
                            n == 0, n == 5, lambda t: pe.wait_ge(res_done[2], 4 * h + (t + 1)), TT)

        @block.scalar
        def _(act):
            steps = [0]

            def chain(ins):
                steps[0] += 1
                ins.then_inc(act_step, 1)
                act.wait_ge(act_step, steps[0])

            act.dma_start(wff[:, :, :], fm_src(w_in, FF, FOX)).then_inc(gate_w_loaded, 16)
            act.dma_start(bf_col[:, :], b_f.rearrange("a h -> h a")).then_inc(gate_w_loaded, 16)
            for r in range(3):
                act.dma_start(side_rows[0:2 * FT, r, :],
                              conv_w[0, r].rearrange("a (j p) -> (a j) p", p=P)).then_inc(rows_loaded, 16)
            act.dma_start(side_rows[0:2 * FT, 3, :], conv_b[0].rearrange("(j p) -> j p", p=P)).then_inc(rows_loaded, 16)
            for r, v in enumerate([ln1_g, ln1_b, ln2_g, ln2_b]):
                act.dma_start(side_rows[0:KT, 4 + r, :], v[0].rearrange("(j p) -> j p", p=P)).then_inc(rows_loaded, 16)
            for r, v in enumerate([lq1, lk1, lq2, lk2]):
                act.dma_start(lam_in[:, r, :], v.to_broadcast([P, HD // 2])).then_inc(lam_loaded, 16)
            act.dma_start(diff_gain[:, :], diff_g.to_broadcast([P, HD])).then_inc(lam_loaded, 16)
            for t in range(MT):
                act.dma_start(mem_tok[:, t, :], mem[0, t * P:(t + 1) * P, :]).then_inc(mem_loaded[t], 16)
            act.preload_act_table_set("natural_log_exp_and_others")

            for n in range(2 * TT):
                t, g = n // 2, n % 2
                act.wait_ge(x_turned, n + 1)
                act.activation(act_hi[:, 4 * g:4 * g + 4, t * P:(t + 1) * P],
                               ps[:, 4 + n % 4, :].rearrange("p (k t) -> p k t", k=4), ACT.Copy).then_inc(x_hi_done, 1)
            act.wait_ge(count_ready, 1)
            act.activation(dil_mask[:, :], prob[:, 0, :], ACT.Ln).then_inc(count_ln, 1)
            act.wait_ge(lam_summed, 2)
            act.activation(lam_s[:, 2:4], lam_s[:, 0:2], ACT.Exp).then_inc(lam_exp, 1)
            act.wait_ge(gate_chain, 4)
            act.activation(fg[:, 2, :], fg[:, 1, :], ACT.Exp, scale=-1.0).then_inc(gate_exp, 1)
            act.wait_ge(gate_exp, 1)
            act.activation(fg[:, 1, :], fg[:, 2, :], ACT.Ln, bias=1.0).then_inc(gate_exp, 1)
            for n in range(16):
                act.wait_ge(dense_done, n + 1)
                scale = 1.0
                if n % 4 < 2:
                    scale = float(np.float32((HD // 2) ** -0.5)) if 4 <= n < 8 else HD ** -0.5
                act.activation(qk_t[:, n, :], ps[:, n % 4, :], ACT.Copy, scale=scale).then_inc(qk_evac, 1)
            act.wait_ge(rows_turned, 1)
            act.activation(conv_cols[:, :, :], ps[:, 6, 0:8 * FT].rearrange("p (r f) -> p r f", r=4), ACT.Copy)\
               .then_inc(cols_ready, 1)
            act.activation(ln_cols[:, :, :], ps[:, 6, 8 * FT:16 * FT].rearrange("p (r f) -> p r f", r=4)[:, :, 0:KT],
                           ACT.Copy).then_inc(cols_ready, 1)
            for n in range(2 * TT):
                h, t = n // TT, n % TT
                act.wait_ge(dense_done, chunks_through("v", 2 * h + 1) + t + 1)
                act.activation(v_tok[:, t, HALF * h:HALF * (h + 1)], ps[:, t, :], ACT.Copy).then_inc(v_evac, 1)
            for n in range(2 * MT):
                t, g = n // 2, n % 2
                act.wait_ge(mem_turned, n + 1)
                act.activation(mem_hi[:, 4 * g:4 * g + 4, t * P:(t + 1) * P],
                               ps[:, 4 + n, :].rearrange("p (k t) -> p k t", k=4), ACT.Copy).then_inc(mem_hi_done, 1)
            for n in range(2 * MT):
                h, t = n // MT, n % MT
                act.wait_ge(dense_done, chunks_through("mk", 2 * h + 1) + t + 1)
                act.activation(mem_tok[:, t, HALF * h:HALF * (h + 1)], ps[:, t, :], ACT.Copy).then_inc(mk_evac, 1)
            for n in range(4):
                act.wait_ge(mk_turned, n + 1)
                act.activation(mem_kt[:, 2 * n:2 * n + 2, :], ps[:, 4 + n, :].rearrange("p (f m) -> p f m", f=2),
                               ACT.Copy).then_inc(mk_ready, 1)
            for h in range(FOX):
                act.wait_ge(forget_spread, h + 1)
                act.activation(scratch[:, h, :], ps[:, 4 + h, :], ACT.Copy).then_inc(forget_k_ready, 1)

            def exps(s):
                hp, i = STEPS[s]
                for j, m in enumerate(maps_of(s)):
                    act.wait_ge(scored, m + 1)
                    row = prob[:, m % 4, 0:(i + 1) * P]
                    act.activation(row, row, ACT.Exp, bias=neg_max[:, m:m + 1], scale=-1.0,
                                   accum_out=den[:, j, s:s + 1]).then_inc(exp_done, 1)

            def keep_probs(s):
                hp, i = STEPS[s]
                turn = TURN_OF_STEP[s]
                act.wait_ge(turned, turn + 1)
                if s >= 2:
                    act.wait_ge(pv_done, s - 1)
                w = (i + 1) * P
                act.activation(prob_t[:, s % 2, 0:w], ps[:, T_BANKS[turn % 2], 0:w], ACT.Copy).then_inc(prob_t_ready, 1)

            exps(0)
            for k in range(N_STEPS + 4):
                if k + 1 < N_STEPS:
                    exps(k + 1)
                if k < N_STEPS:
                    keep_probs(k)
                if k >= 5 and (k - 5) % TT == 0 and (k - 5) // TT < DIFF:
                    h = (k - 5) // TT
                    act.wait_ge(rms_summed, h + 1)
                    act.wait_ge(eps_set, 1)
                    chain(act.activation(rms_s[:, 1, h, :], rms_s[:, 0, h, :], ACT.Ln, scale=1.0 / HD, bias=eps[:, :]))
                    act.activation(rms_s[:, 2, h, :], rms_s[:, 1, h, :], ACT.Exp, scale=-0.5).then_inc(rms_scaled, 1)
                if k >= PAIR_LAG and (k - PAIR_LAG) % 8 == 0:
                    p = (k - PAIR_LAG) // 8
                    turn = TURN_OF_PAIR[p]
                    act.wait_ge(turned, turn + 1)
                    act.activation(act_hi[:, HEAD_ORDER[2 * p] // 2, :], ps[:, T_BANKS[turn % 2], :],
                                   ACT.Copy).then_inc(o_hi_done, 1)

            def ln_rstd(n):
                for t in range(TT):
                    act.wait_ge(var_ready[n], t + 1)
                    chain(act.activation(ln_var[:, t:t + 1], mean_var[:, t, 1:2], ACT.Ln, bias=eps[:, :]))
                    act.activation(rstd[:, t:t + 1], ln_var[:, t:t + 1], ACT.Exp, scale=-0.5).then_inc(rstd_ready[n], 1)

            def ln_high(n):
                def apply(k):
                    act.wait_ge(z_turned[n], k + 1)
                    if k >= 4:
                        act.wait_ge(z_lo_done[n], k - 3)
                    act.activation(scratch[:, k % 4, :], ps[:, 4 + k % 4, :], ACT.Identity,
                                   scale=ln_cols[:, 2 * n, k:k + 1], bias=ln_cols[:, 2 * n + 1, k:k + 1])\
                       .then_inc(y_by_act[n], 1)

                apply(0)
                for k in range(KT):
                    if k % 2 == 1 and k + 1 < KT:
                        apply(k + 1)
                    act.wait_ge([y_by_act, y_by_vec][k % 2][n], k // 2 + 1)
                    act.activation(act_hi[:, k, :], scratch[:, k % 4, :], ACT.Copy).then_inc(z_hi_done[n], 1)

            ln_rstd(0)
            for n in range(2 * MT):
                h, t = n // MT, n % MT
                act.wait_ge(dense_done, chunks_through("mv", 2 * h + 1) + t + 1)
                act.activation(mem_v[:, t, HALF * h:HALF * (h + 1)], ps[:, t, :], ACT.Copy).then_inc(mv_evac, 1)
            ln_high(0)
            for n in range(KT):
                act.wait_ge(dense_done, CHUNK0["mq"] + n + 1)
                act.activation(xq_t[:, n, :], ps[:, n % 4, :], ACT.Copy, scale=(D // MEM_HEADS) ** -0.5)\
                   .then_inc(mq_evac, 1)

            N_X = MEM_HEADS * TT

            def x_exp(c):
                act.wait_ge(x_maxed, c + 1)
                if c >= 4:
                    act.wait_ge(xp_turned, c - 3)
                act.activation(xp[:, c % 4, :], ps[:, 4 + c % 2, 0:MEM], ACT.Exp, bias=x_neg_max[:, c:c + 1],
                               accum_out=x_den[:, c:c + 1]).then_inc(x_exp_done, 1)

            def x_keep(pair):
                h, i = pair // 2, 2 * (pair % 2)
                act.wait_ge(xp_turned, 2 * pair + 2)
                if h >= 2:
                    act.wait_ge(xo_done, 2 * (h - 1))
                for t in range(2):
                    ins = act.activation(xp_t[:, h % 2, :, (i + t) * P:(i + t + 1) * P],
                                         ps[:, 6 + pair % 2, t * MT * P:(t + 1) * MT * P]
                                         .rearrange("p (m q) -> p m q", m=MT), ACT.Copy)
                ins.then_inc(xp_t_ready, 1)

            def xo_high(h):
                for f in range(2):
                    act.wait_ge(xo_done, 2 * h + f + 1)
                    act.activation(act_hi[:, 2 * h + f, :], ps[:, 2 * (h % 2) + f, :], ACT.Copy).then_inc(xo_hi_done, 1)

            x_exp(0)
            for c in range(N_X + 2):
                if c + 1 < N_X:
                    x_exp(c + 1)
                if c < N_X and c % 2 == 1:
                    x_keep(c // 2)
                if c >= TT + 1 and (c - TT - 1) % TT == 0:
                    xo_high((c - TT - 1) // TT)
            ln_rstd(1)
            ln_high(1)

            act.wait_ge(z_lo_done[1], KT)
            act.sem_inc(gelu_done, 2)
            act.sem_inc(gated, 2)
            with act.Fori(0, FT // 2) as t:
                def tap2(q, tile0):
                    act.wait_ge(dense_done, 4 * t + (CHUNK0["up"] + q + 1))
                    if q < 2:
                        act.wait_ge(gelu_done, 2 * t + (q + 1))
                    else:
                        act.wait_ge(gated, 2 * t + (q - 1))
                    act.wait_ge(cols_ready, 2)
                    act.activation(scratch[:, q, :], ps[:, q, :], ACT.Identity,
                                   scale=conv_cols[:, 2, bass.ds(2 * t + tile0, 1)],
                                   bias=conv_cols[:, 3, bass.ds(2 * t + tile0, 1)]).then_inc(tap2_done, 1)

                tap2(0, 0)
                tap2(1, 1)
                for q in range(2):
                    act.wait_ge(conv_done, 4 * t + (4 + q + 1))
                    act.wait_ge(gated, 2 * t + (q + 1))
                    act.activation(side[:, q, :], scratch[:, q, :], ACT.Gelu_apprx_tanh).then_inc(gelu_done, 1)
                tap2(2, FT)
                tap2(3, FT + 1)
                for q in range(2):
                    act.wait_ge(gated, 2 * t + (2 + q + 1))
                    act.wait_ge(cols_ready, 2)
                    act.activation(gate_hi[:, bass.ds(2 * t + q, 1), :].rearrange("p a b -> p (a b)"),
                                   side[:, 2 + q, :], ACT.Copy).then_inc(gate_hi_done, 1)
            ln_rstd(2)

        @block.vector
        def _(vec):
            steps = [0]

            def chain(ins):
                steps[0] += 1
                ins.then_inc(vec_step, 1)
                vec.wait_ge(vec_step, steps[0])

            def sub_hi(dst, src, hi):
                return vec.tensor_tensor(dst, src, hi.bitcast(F32), ALU.subtract)

            vec.wait_ge(gate_w_loaded, 32)
            vec.tensor_copy(wff_hi[:, :, :], wff[:, :, :]).then_inc(gate_chain, 1)
            vec.wait_ge(gate_chain, 1)
            sub_hi(wff_lo[:, :, :], wff[:, :, :], wff_hi[:, :, :]).then_inc(gate_chain, 1)
            for n in range(2 * TT):
                t, g = n // 2, n % 2
                vec.wait_ge(x_hi_done, n + 1)
                sub_hi(act_lo[:, 4 * g:4 * g + 4, t * P:(t + 1) * P],
                       ps[:, 4 + n % 4, :].rearrange("p (k t) -> p k t", k=4),
                       act_hi[:, 4 * g:4 * g + 4, t * P:(t + 1) * P]).then_inc(x_lo_done, 1)
            masks = [0]

            def mask_chain(ins):
                masks[0] += 1
                ins.then_inc(mask_step, 1)
                vec.wait_ge(mask_step, masks[0])

            count, m4, m16 = prob[:, 0, :], prob[:, 1, :], prob[:, 2, :]
            dist_i = prob[:, 3, :].bitcast(I32)
            vec.wait_ge(masks_made, 4)
            mask_chain(vec.tensor_scalar(m4.bitcast(I32), dist_i, 3, None, ALU.bitwise_and))
            mask_chain(vec.tensor_scalar(m16.bitcast(I32), dist_i, 15, None, ALU.bitwise_and))
            mask_chain(vec.tensor_scalar(dil_mask[:, :], m4.bitcast(I32), 0.0, None, ALU.is_equal))
            mask_chain(vec.scalar_tensor_tensor(count, dist[:, :], float(P), dil_mask[:, :], ALU.is_le, ALU.add))
            mask_chain(vec.scalar_tensor_tensor(m4, m16.bitcast(I32), 0.0, count, ALU.is_equal, ALU.add))
            vec.tensor_scalar(count, m4, 1.0, None, ALU.max).then_inc(count_ready, 1)
            mask_chain(vec.tensor_scalar(m16, m4, 0.0, NEG, ALU.is_equal, ALU.mult))
            vec.wait_ge(count_ln, 1)
            mask_chain(vec.tensor_tensor(dil_mask[:, :], dil_mask[:, :], causal[:, :], ALU.add))
            vec.tensor_tensor(dil_mask[:, :], dil_mask[:, :], m16, ALU.add).then_inc(dil_mask_made, 1)
            vec.wait_ge(lam_loaded, 16 * 5)
            for n in range(2):
                vec.tensor_tensor_reduce(lam_in[:, 2 * n, :], lam_in[:, 2 * n, :], lam_in[:, 2 * n + 1, :], 1.0, 0.0,
                                         ALU.mult, ALU.add, lam_s[:, n:n + 1]).then_inc(lam_summed, 1)
            vec.wait_ge(ff_summed, 1)
            vec.wait_ge(dil_mask_made, 1)
            vec.tensor_scalar(fg[:, 0, :], ps[0:FOX, 4, :], bf_col[:, :], None, ALU.add).then_inc(gate_chain, 1)
            vec.wait_ge(gate_chain, 3)
            vec.scalar_tensor_tensor(fg[:, 1, :], fg[:, 0, :], -1.0, fg[:, 0, :], ALU.mult, ALU.max)\
               .then_inc(gate_chain, 1)
            vec.wait_ge(gate_exp, 2)
            vec.scalar_tensor_tensor(fg[:, 3, :], fg[:, 0, :], 0.0, fg[:, 1, :], ALU.min, ALU.subtract)\
               .then_inc(gate_chain, 1)
            vec.wait_ge(gate_chain, 5)
            vec.tensor_tensor_scan(fg[:, 2, :], fg[:, 3, :], fg[:, 3, :], 0.0, ALU.add, ALU.bypass)\
               .then_inc(gate_chain, 1)
            vec.wait_ge(lam_exp, 1)
            chain(vec.tensor_tensor(lam_s[:, 4:5], lam_s[:, 3:4], lam_s[:, 2:3], ALU.subtract))
            chain(vec.tensor_scalar(lam_s[:, 5:6], lam_s[:, 4:5], -LAM_INIT, None, ALU.add))
            chain(vec.tensor_scalar(diff_gain[:, :], diff_gain[:, :], 1.0 - LAM_INIT, None, ALU.mult))
            vec.memset(eps[:, :], LN_EPS).then_inc(eps_set, 1)
            vec.wait_ge(forget_turned, 1)
            vec.tensor_copy(forget_q[:, :, :], ps[:, 5, 0:TT * FOX].rearrange("p (i h) -> p i h", i=TT))\
               .then_inc(forget_q_ready, 1)
            for n in range(2 * MT):
                t, g = n // 2, n % 2
                vec.wait_ge(mem_hi_done, n + 1)
                sub_hi(mem_lo[:, 4 * g:4 * g + 4, t * P:(t + 1) * P],
                       ps[:, 4 + n, :].rearrange("p (k t) -> p k t", k=4),
                       mem_hi[:, 4 * g:4 * g + 4, t * P:(t + 1) * P]).then_inc(mem_lo_done, 1)

            def score(s):
                hp, i = STEPS[s]
                n = bias_item(s)
                w = (i + 1) * P
                lo = 0 if is_fox(hp) else SEQ - w
                vec.wait_ge(bias_made, n + 1)
                for m in maps_of(s):
                    vec.wait_ge(qk_done, m + 1)
                    if m < 4:
                        vec.wait_ge(forget_spread, FOX)
                    else:
                        before = next(r for r in range(N_STEPS) if m - 4 in maps_of(r))
                        vec.wait_ge(turned, TURN_OF_STEP[before] + 1)
                    vec.tensor_tensor_reduce(prob[:, m % 4, 0:w], ps[:, S_BANKS[m % 4], 0:w],
                                             side[:, n % 4, lo:lo + w], -1.0, BIG, ALU.add, ALU.min,
                                             neg_max[:, m:m + 1]).then_inc(scored, 1)

            def mix(s):
                hp, i = STEPS[s]
                m0, m1 = maps_of(s)
                w = (i + 1) * P
                vec.wait_ge(exp_done, m1 + 1)
                chain(vec.reciprocal(mix_s[:, 0, s:s + 1], den[:, 1, s:s + 1]))
                chain(vec.scalar_tensor_tensor(mix_s[:, 1, s:s + 1], den[:, 0, s:s + 1], mix_s[:, 0, s:s + 1],
                                               lam_s[:, 5:6], ALU.mult, ALU.mult))
                vec.scalar_tensor_tensor(prob[:, m0 % 4, 0:w], prob[:, m1 % 4, 0:w], mix_s[:, 1, s:s + 1],
                                         prob[:, m0 % 4, 0:w], ALU.mult, ALU.add).then_inc(mixed, 1)

            def spread(ap):
                return ap.rearrange("p (i o) -> p i o", o=1).to_broadcast([P, TT, HD])

            def o_half(hp):
                return o_tok[:, :, (hp % 2) * HD:(hp % 2 + 1) * HD]

            def norm_output(hp):
                rden = den[:, 0, TT * hp:TT * (hp + 1)]
                vec.wait_ge(pv_done, TT * (hp + 1))
                chain(vec.reciprocal(rden, rden))
                if hp >= 2 and hp % 2 == 0:
                    vec.wait_ge(turned, TURN_OF_PAIR[hp // 2 - 1] + 1)
                vec.tensor_tensor(o_half(hp), ps[:, O_BANKS[hp % 2], 0:TT * HD].rearrange("p (i d) -> p i d", i=TT),
                                  spread(rden), ALU.mult).then_inc(o_normed, 1)
                if is_diff(hp):
                    vec.wait_ge(o_normed, hp + 1)
                    sq = ps[:, O_BANKS[hp % 2], TT * HD:2 * TT * HD].rearrange("p (i d) -> p i d", i=TT)
                    chain(vec.tensor_tensor(sq, o_half(hp), o_half(hp), ALU.mult))
                    vec.tensor_reduce(rms_s[:, 0, hp, :], sq, AX.X, ALU.add).then_inc(rms_summed, 1)

            def rms_output(hp):
                vec.wait_ge(rms_scaled, hp + 1)
                chain(vec.tensor_tensor(o_half(hp), o_half(hp), spread(rms_s[:, 2, hp, :]), ALU.mult))
                vec.tensor_tensor(o_half(hp), o_half(hp),
                                  diff_gain[:, :].rearrange("p (o d) -> p o d", o=1).to_broadcast([P, TT, HD]),
                                  ALU.mult).then_inc(o_rmsed, 1)

            score(0)
            for k in range(N_STEPS + 4):
                if k + 1 < N_STEPS:
                    score(k + 1)
                if k < N_STEPS and is_diff(STEPS[k][0]):
                    mix(k)
                if k >= 5 and (k - 5) % TT == 0:
                    if (k - 5) // TT < HEADS:
                        norm_output((k - 5) // TT)
                if k >= 6 and (k - 6) % TT == 0 and (k - 6) // TT < DIFF:
                    rms_output((k - 6) // TT)
                if k >= PAIR_LAG and (k - PAIR_LAG) % 8 == 0:
                    p = (k - PAIR_LAG) // 8
                    kt = HEAD_ORDER[2 * p] // 2
                    vec.wait_ge(o_hi_done, p + 1)
                    sub_hi(act_lo[:, kt, :], ps[:, T_BANKS[TURN_OF_PAIR[p] % 2], :], act_hi[:, kt, :])\
                       .then_inc(o_lo_done, 1)

            def add_residual(n, phase, units, h, t, inside):
                x_half = x_tok[:, t, HALF * h:HALF * (h + 1)]
                vec.wait_ge(dense_done, chunks_through(phase, units * h + units - 1) + t + 1)
                vec.scalar_tensor_tensor(x_half, x_half, ALPHA, ps[:, t, :], ALU.mult, ALU.add).then_inc(res_done[n], 1)
                vec.wait_ge(res_done[n], TT + TT * h + t + 1)
                chain(vec.bn_stats(stats[:, t, h, :], x_half))

            def find_var(n, t):
                vec.bn_aggr(mean_var[:, t, :], stats[:, t, :, :].rearrange("p a b -> p (a b)")).then_inc(var_ready[n], 1)

            def layer_norm(n, phase):
                for t in range(TT):
                    add_residual(n, phase, 2, 0, t, 0)

                def normalise(t):
                    vec.wait_ge(rstd_ready[n], t + 1)
                    vec.tensor_scalar(x_tok[:, t, :], x_tok[:, t, :], mean_var[:, t, 0:1], rstd[:, t:t + 1],
                                      ALU.subtract, ALU.mult).then_inc(z_ready[n], 1)

                for t in range(TT):
                    add_residual(n, phase, 2, 1, t, 0)
                    find_var(n, t)
                    if t >= 1:
                        normalise(t - 1)
                normalise(TT - 1)
                def apply(k):
                    vec.wait_ge(z_turned[n], k + 1)
                    if k >= 4:
                        vec.wait_ge(z_lo_done[n], k - 3)
                    vec.tensor_scalar(scratch[:, k % 4, :], ps[:, 4 + k % 4, :], ln_cols[:, 2 * n, k:k + 1],
                                      ln_cols[:, 2 * n + 1, k:k + 1], ALU.mult, ALU.add).then_inc(y_by_vec[n], 1)

                apply(1)
                for k in range(KT):
                    if k % 2 == 0 and 2 <= k:
                        apply(k + 1)
                    vec.wait_ge(z_hi_done[n], k + 1)
                    sub_hi(act_lo[:, k, :], scratch[:, k % 4, :], act_hi[:, k, :]).then_inc(z_lo_done[n], 1)
                vec.wait_ge(gains_loaded[n], 32)
                for t in range(TT):
                    chain(vec.tensor_tensor(x_tok[:, t, :], x_tok[:, t, :], side_gain[:, 0, :], ALU.mult))
                    vec.tensor_tensor(x_tok[:, t, :], x_tok[:, t, :], side_gain[:, 1, :], ALU.add)\
                       .then_inc(ln_applied[n], 1)

            layer_norm(0, "wo")

            N_X = MEM_HEADS * TT

            def x_max(c):
                vec.wait_ge(xs_done, c + 1)
                vec.tensor_reduce(x_neg_max[:, c:c + 1], ps[:, 4 + c % 2, 0:MEM], AX.X, ALU.max,
                                  negate=True).then_inc(x_maxed, 1)

            def x_scale(c):
                vec.wait_ge(x_exp_done, c + 1)
                chain(vec.reciprocal(x_rden[:, c:c + 1], x_den[:, c:c + 1]))
                vec.tensor_scalar(xp[:, c % 4, :], xp[:, c % 4, :], x_rden[:, c:c + 1], None, ALU.mult)\
                   .then_inc(x_scaled, 1)

            x_max(0)
            for c in range(N_X + 2):
                if c + 1 < N_X:
                    x_max(c + 1)
                if c < N_X:
                    x_scale(c)
                if c >= TT + 1 and (c - TT - 1) % TT == 0:
                    h = (c - TT - 1) // TT
                    for f in range(2):
                        vec.wait_ge(xo_hi_done, 2 * h + f + 1)
                        sub_hi(act_lo[:, 2 * h + f, :], ps[:, 2 * (h % 2) + f, :], act_hi[:, 2 * h + f, :])\
                           .then_inc(xo_lo_done, 1)
            layer_norm(1, "mo")
            vec.wait_ge(ln_applied[1], TT)

            vec.sem_inc(gate_lo_done, 2)
            with vec.Fori(0, FT // 2) as t:
                def older_taps(q, tile0):
                    vec.wait_ge(tap2_done, 4 * t + (q + 1))
                    vec.scalar_tensor_tensor(scratch[:, q, 1:SEQ], ps[:, q, 0:SEQ - 1],
                                             conv_cols[:, 1, bass.ds(2 * t + tile0, 1)], scratch[:, q, 1:SEQ],
                                             ALU.mult, ALU.add).then_inc(tap1_done, 1)
                    vec.wait_ge(tap1_done, 4 * t + (q + 1))
                    vec.scalar_tensor_tensor(scratch[:, q, 2:SEQ], ps[:, q, 0:SEQ - 2],
                                             conv_cols[:, 0, bass.ds(2 * t + tile0, 1)], scratch[:, q, 2:SEQ],
                                             ALU.mult, ALU.add).then_inc(conv_done, 1)

                for q, tile0 in enumerate([0, 1, FT, FT + 1]):
                    older_taps(q, tile0)
                for q in range(2):
                    vec.wait_ge(gelu_done, 2 * t + (2 + q + 1))
                    vec.wait_ge(conv_done, 4 * t + (4 + q + 3))
                    vec.wait_ge(gate_lo_done, 2 * t + (q + 1))
                    vec.tensor_tensor(side[:, 2 + q, :], side[:, q, :], scratch[:, 2 + q, :], ALU.mult)\
                       .then_inc(gated, 1)
                for q in range(2):
                    vec.wait_ge(gate_hi_done, 2 * t + (q + 1))
                    tile = bass.ds(2 * t + q, 1)
                    vec.tensor_tensor(gate_lo[:, tile, :].rearrange("p a b -> p (a b)"), side[:, 2 + q, :],
                                      gate_hi[:, tile, :].rearrange("p a b -> p (a b)").bitcast(F32),
                                      ALU.subtract).then_inc(gate_lo_done, 1)

            for t in range(TT):
                add_residual(2, "down", 6, 0, t, 0)
            vec.wait_ge(gains_loaded[2], 32)
            for t in range(TT):
                add_residual(2, "down", 6, 1, t, 0)
                find_var(2, t)
                vec.wait_ge(var_ready[2], t + 1)
                chain(vec.scalar_tensor_tensor(x_tok[:, t, :], x_tok[:, t, :], mean_var[:, t, 0:1],
                                               side_gain[:, 0, :], ALU.subtract, ALU.mult))
                vec.wait_ge(rstd_ready[2], t + 1)
                vec.scalar_tensor_tensor(x_tok[:, t, :], x_tok[:, t, :], rstd[:, t:t + 1], side_gain[:, 1, :],
                                         ALU.mult, ALU.add).then_inc(ln_applied[2], 1)


_INS = ["x", "mem", "w_in", "b_f", "lambda_q1", "lambda_k1", "lambda_q2", "lambda_k2", "diff_norm_g", "w_o",
        "ln1_g", "ln1_b", "w_mq", "w_mkv", "w_mo", "ln2_g", "ln2_b", "w_up", "conv_w", "conv_b", "w_down",
        "ln3_g", "ln3_b"]
_OUTS = [((1, SEQ, D), "float32")]


def kernel(**inputs):
    import numpy as _np
    import concourse.bacc as _bacc
    from concourse import mybir as _mybir
    from concourse.bass_utils import run_bass_kernel_spmd as _run

    nc = _bacc.Bacc("TRN2", target_bir_lowering=False, num_devices=1)
    arrays, args = {}, []
    for name in _INS:
        a = _np.ascontiguousarray(inputs[name])
        arrays[f"in_{name}_dram"] = a
        args.append(nc.dram_tensor(f"in_{name}_dram", a.shape, _mybir.dt.from_np(a.dtype), kind="ExternalInput").ap())
    for i, (shape, dtype) in enumerate(_OUTS):
        dt = _mybir.dt.from_np(_np.dtype(dtype))
        args.append(nc.dram_tensor(f"out_{i}_dram", shape, dt, kind="ExternalOutput").ap())
    build_layer(nc, *args)
    r = _run(nc, [arrays], core_ids=[0])
    return r.results[0]["out_0_dram"]
```

```python
from contextlib import ExitStack

import numpy as np

import concourse.bass as bass
from concourse import mybir

F32 = mybir.dt.float32
F32R = mybir.dt.float32r
I32 = mybir.dt.int32
ALU = mybir.AluOpType
ACT = mybir.ActivationFunctionType
AX = mybir.AxisListType

P = 128
SEQ = 512
D = 1024
MEM = 256
HD = 64
FOX, DIFF, DIL = 4, 4, 8
FOX_W, DIFF_W, DIL_W = FOX * HD, DIFF * HD, DIL * HD
HEADS = FOX + DIFF + DIL
D_FF = 2816
MEM_HEADS = 4
TT = SEQ // P
KT = D // P
MT = MEM // P
FT = D_FF // P
UNIT = 2048
VEC_PART = 1536
HALF = 512
ALPHA = 2.0 ** 0.25
LN_EPS = 1e-5
X_SCALE = (D // MEM_HEADS) ** -0.5
NEG = -1e30
BIG = 3e38
LAM_INIT = 0.2
N_SLOPES = DIFF + DIL
SLOPES = [float(np.float32(2.0 ** (-8.0 * j / N_SLOPES))) for j in range(1, N_SLOPES + 1)]
DIFF_SLOPES = SLOPES[::N_SLOPES // DIFF]
DIL_SLOPES = [s for j, s in enumerate(SLOPES) if j % (N_SLOPES // DIFF)]

PHASES = [("v", "tm", 4, 4), ("qk", "fm", 8, 2), ("mv", "tm", 4, 2), ("wo", "tm", 4, 4),
          ("mk", "tm", 4, 2), ("mq", "fm", 4, 2), ("mo", "tm", 4, 4), ("up", "fm", 2 * FT // 2, 2),
          ("down", "tm", 12, 4)]
UNIT0, CHUNK0, CHUNKS = {}, {}, {}
_u = _c = 0
for _name, _kind, _n, _ch in PHASES:
    UNIT0[_name], CHUNK0[_name], CHUNKS[_name] = _u, _c, _ch
    _u, _c = _u + _n, _c + _n * _ch
N_UNITS = _u
SHARED = [UNIT0["v"], UNIT0["v"] + 1, UNIT0["mk"] + 2, UNIT0["mk"] + 3]
DOWN_KT = [4, 4, 3, 3, 4, 4]
DOWN_K0 = [0, 4, 8, 11, 14, 18]


def chunks_through(phase, n):
    return CHUNK0[phase] + CHUNKS[phase] * n


HEAD_ORDER = [FOX + h for h in range(DIFF)] + list(range(FOX)) + list(range(FOX + DIFF, HEADS))
STEPS = [(hp, i) for hp in range(HEADS) for i in range(TT)]
N_STEPS = len(STEPS)


def is_diff(hp):
    return hp < DIFF


def is_fox(hp):
    return DIFF <= hp < DIFF + FOX


def maps_of(s):
    return [2 * s, 2 * s + 1] if is_diff(STEPS[s][0]) else [DIFF * TT + s]


N_MAPS = maps_of(N_STEPS - 1)[-1] + 1


def bias_item(s):
    hp, i = STEPS[s]
    if is_diff(hp):
        return hp
    if is_fox(hp):
        return DIFF + (hp - DIFF) * TT + i
    return DIFF + FOX * TT + hp - DIFF - FOX


N_ITEMS = bias_item(N_STEPS - 1) + 1
LAST_MAP_OF_ITEM = [max(maps_of(s)[-1] for s in range(N_STEPS) if bias_item(s) == n) for n in range(N_ITEMS)]
HEAD_BLOCKS = TT * (TT + 1) // 2


def prob_place(m):
    s = next(t for t in range(N_STEPS) if m in maps_of(t))
    hp, i = STEPS[s]
    slot = maps_of(s).index(m) if is_diff(hp) else (hp - DIFF) % 2
    before = s - TT if is_diff(hp) or hp == DIFF else s - 2 * TT
    return (slot * HEAD_BLOCKS + i * (i + 1) // 2) * P, before


FILL = 3
FILL_STARTS = [0, 9, 38, 47]
FILL_STEPS = 3 * KT // FILL
AHEAD = 2
PAIR_LAG = 10
TURN_OF_STEP, TURN_OF_PAIR = {}, {}
for _k in range(N_STEPS):
    TURN_OF_STEP[_k] = len(TURN_OF_STEP) + len(TURN_OF_PAIR)
    if _k >= PAIR_LAG and (_k - PAIR_LAG) % 8 == 0 and (_k - PAIR_LAG) // 8 < DIFF // 2:
        TURN_OF_PAIR[(_k - PAIR_LAG) // 8] = len(TURN_OF_STEP) + len(TURN_OF_PAIR)
STEP_OF_TURN = {t: s for s, t in TURN_OF_STEP.items()}
PAIR_OF_TURN = {t: p for p, t in TURN_OF_PAIR.items()}
S_BANKS = [4, 5, 0]
FILL_BANK = 1
T_BANKS = [6, 7]
O_BANKS = [2, 3]
X_S_BANKS = [4, 5, 2, 3]
X_O_BANK = [0, 0, 0, 4]
X_O_LAG = 2
X_AHEAD = 2


def qk_place(hp, j):
    head = HEAD_ORDER[hp]
    if is_diff(hp):
        h = head - FOX
        return 4 + h // 2, 6 + h // 2, (h % 2) * HD + j * HD // 2, HD // 2
    if is_fox(hp):
        return head // 2, 2 + head // 2, (head % 2) * HD, HD
    g = head - FOX - DIFF
    tile = 8 + 4 * (g // 4) + (g % 4) // 2
    return tile, tile + 2, (g % 2) * HD, HD


def build_layer(nc, x, mem, w_in, b_f, lq1, lk1, lq2, lk2, diff_g, w_o, ln1_g, ln1_b, w_mq, w_mkv,
                w_mo, ln2_g, ln2_b, w_up, conv_w, conv_b, w_down, ln3_g, ln3_b, out):
    ctx = ExitStack()
    attention_memory = ExitStack()
    memory_memory = ExitStack()

    def sb(name, shape, dt=F32, stack=ctx):
        return stack.enter_context(nc.sbuf_tensor(name, shape, dt))

    def sem(name):
        return ctx.enter_context(nc.semaphore(name))

    with ctx:
        x_tok = sb("x_tok", [P, TT, D])
        act_hi = sb("act_hi", [P, KT, SEQ], F32R)
        act_lo = sb("act_lo", [P, KT, SEQ], F32R)
        raw = sb("raw", [P, 2, UNIT])
        w_hi = sb("w_hi", [P, 2, UNIT], F32R)
        w_lo = sb("w_lo", [P, 2, UNIT], F32R)
        scratch = sb("scratch", [P, 4, HALF])
        side = sb("side", [P, 4, HALF])
        ident = sb("ident", [P, P])
        conv_cols = sb("conv_cols", [P, 4, 2 * FT])
        ln_cols = sb("ln_cols", [P, 4, KT])
        eps = sb("eps", [P, 1])
        stats = sb("stats", [P, TT, 2, 6])
        mean_var = sb("mean_var", [P, TT, 2])
        ln_var = sb("ln_var", [P, TT])
        rstd = sb("rstd", [P, TT])
        neg_mean = sb("neg_mean", [P, TT])
        ln_shift = sb("ln_shift", [P, TT])
        mem_hi = sb("mem_hi", [P, KT, MEM], F32R, memory_memory)
        mem_lo = sb("mem_lo", [P, KT, MEM], F32R, memory_memory)
        mem_v = sb("mem_v", [P, MT, D], F32, memory_memory)
        am = attention_memory
        qk_t = sb("qk_t", [P, 16, SEQ], F32, am)
        v_tok = sb("v_tok", [P, TT, D], F32, am)
        prob = sb("prob", [P, 2 * HEAD_BLOCKS * P], F32, am)
        prob_t = sb("prob_t", [P, 2, SEQ], F32, am)
        head_ones = sb("head_ones", [P, P], F32, am)
        dist = sb("dist", [P, SEQ], F32, am)
        causal = sb("causal", [P, SEQ], F32, am)
        dil_mask = sb("dil_mask", [P, SEQ], F32, am)
        lam_s = sb("lam_s", [P, 6], F32, am)
        diff_gain = sb("diff_gain", [P, 1], F32, am)
        neg_max = sb("neg_max", [P, N_MAPS], F32, am)
        den = sb("den", [P, 2, N_STEPS], F32, am)
        mix_s = sb("mix_s", [P, 2, DIFF * TT], F32, am)
        forget_q = sb("forget_q", [P, TT, FOX], F32, am)
        wff = sb("wff", [P, KT, FOX], F32, am)
        wff_hi = sb("wff_hi", [P, KT, FOX], F32R, am)
        wff_lo = sb("wff_lo", [P, KT, FOX], F32R, am)
        bf_col = sb("bf_col", [FOX, 1], F32, am)
        am.close()
        cross = ExitStack()
        mem_kt_hi = sb("mem_kt_hi", [P, KT, MEM], F32R, cross)
        mem_kt_lo = sb("mem_kt_lo", [P, KT, MEM], F32R, cross)
        xq_hi = sb("xq_hi", [P, KT, SEQ], F32R, cross)
        xq_lo = sb("xq_lo", [P, KT, SEQ], F32R, cross)
        xp = sb("xp", [P, 4, MEM], F32, cross)
        xp_t_hi = sb("xp_t_hi", [P, 2, MT, SEQ], F32R, cross)
        x_neg_max = sb("x_neg_max", [P, MEM_HEADS * TT], F32, cross)
        x_den = sb("x_den", [P, MEM_HEADS * TT], F32, cross)
        x_rden = sb("x_rden", [P, MEM_HEADS * TT], F32, cross)
        with ExitStack() as keys:
            mem_k = sb("mem_k", [P, MT, D], F32, keys)
        xp_t_lo = sb("xp_t_lo", [P, 2, MT, SEQ], F32R, cross)
        cross.close()
        memory_memory.close()
        gate_hi = sb("gate_hi", [P, FT, SEQ], F32R)
        gate_lo = sb("gate_lo", [P, FT, SEQ], F32R)

        ps = ctx.enter_context(nc.psum_tensor("ps", [P, 8, HALF], F32))

        mem_v_hi = mem_hi[:, :, :].rearrange("p k m -> p (k m)").rearrange("p (m d) -> p m d", m=MT)
        mem_v_lo = mem_lo[:, :, :].rearrange("p k m -> p (k m)").rearrange("p (m d) -> p m d", m=MT)
        mem_tok = scratch[:, :, :].rearrange("p a b -> p (a b)").rearrange("p (m d) -> p m d", m=MT)
        side_rows = side[:, :, :].rearrange("p a b -> p (a b)").rearrange("p (r f) -> p r f", f=P)
        lam_in = side_rows[:, 8, :].rearrange("p (r d) -> p r d", r=4)
        side_gain = side[:, :, :].rearrange("p a b -> p (a b)").rearrange("p (m d) -> p m d", m=2)

        def rms_t(p):
            return qk_t[:, 4 + p, :]

        prob_rows = prob[:, 0:4 * SEQ].rearrange("p (a b) -> p a b", a=4)
        fg = prob_rows[0:FOX, :, :]
        fsel = prob_t[0:FOX, 0, :].rearrange("p (h q) -> p h q", h=FOX)

        x_loaded = [sem(f"x_loaded{t}") for t in range(TT)]
        mem_loaded = [sem(f"mem_loaded{t}") for t in range(MT)]
        gate_w_loaded = sem("gate_w_loaded")
        rows_loaded = sem("rows_loaded")
        lam_loaded = sem("lam_loaded")
        raw_loaded = [sem(f"raw_loaded{s}") for s in range(2)]
        gains_loaded = [sem(f"gains_loaded{n}") for n in range(3)]
        stored = sem("stored")
        ident_made = sem("ident_made")
        masks_zeroed = sem("masks_zeroed")
        masks_made = sem("masks_made")
        ones_made = sem("ones_made")
        hi_split = sem("hi_split")
        split_done = sem("split_done")
        vec_rounded = sem("vec_rounded")
        vec_split = sem("vec_split")
        bias_scaled = sem("bias_scaled")
        bias_made = sem("bias_made")
        dense_done = sem("dense_done")
        x_turned = sem("x_turned")
        x_hi_done = sem("x_hi_done")
        x_lo_done = sem("x_lo_done")
        ff_summed = sem("ff_summed")
        gate_chain = sem("gate_chain")
        gate_exp = sem("gate_exp")
        forget_turned = sem("forget_turned")
        forget_q_ready = sem("forget_q_ready")
        forget_spread = sem("forget_spread")
        forget_k_ready = sem("forget_k_ready")
        rows_turned = sem("rows_turned")
        cols_ready = sem("cols_ready")
        lam_exp = sem("lam_exp")
        qk_evac = sem("qk_evac")
        v_evac = sem("v_evac")
        mk_evac = sem("mk_evac")
        mv_half = sem("mv_half")
        mv_evac = sem("mv_evac")
        mq_evac = sem("mq_evac")
        mem_turned = sem("mem_turned")
        mem_hi_done = sem("mem_hi_done")
        mem_lo_done = sem("mem_lo_done")
        mk_turned = sem("mk_turned")
        mk_ready = sem("mk_ready")
        qk_done = sem("qk_done")
        scored = sem("scored")
        exp_done = sem("exp_done")
        mixed = sem("mixed")
        turned = sem("turned")
        prob_t_ready = sem("prob_t_ready")
        pv_done = sem("pv_done")
        normed = sem("normed")
        squared = sem("squared")
        rms_summed = sem("rms_summed")
        rms_scaled = sem("rms_scaled")
        o_rmsed = sem("o_rmsed")
        o_hi_done = sem("o_hi_done")
        o_lo_done = sem("o_lo_done")
        res_done = [sem(f"res_done{n}") for n in range(3)]
        var_ready = [sem(f"var_ready{n}") for n in range(3)]
        rstd_ready = [sem(f"rstd_ready{n}") for n in range(3)]
        z_ready = [sem(f"z_ready{n}") for n in range(2)]
        z_turned = [sem(f"z_turned{n}") for n in range(2)]
        y_by_act = [sem(f"y_by_act{n}") for n in range(2)]
        y_by_vec = [sem(f"y_by_vec{n}") for n in range(2)]
        z_hi_done = [sem(f"z_hi_done{n}") for n in range(2)]
        z_lo_done = [sem(f"z_lo_done{n}") for n in range(2)]
        ln_applied = [sem(f"ln_applied{n}") for n in range(3)]
        neg_mean_ready = sem("neg_mean_ready")
        last_z_ready = sem("last_z_ready")
        last_gained = sem("last_gained")
        third_gained = sem("third_gained")
        third_done = sem("third_done")
        last_half_gained = sem("last_half_gained")
        last_half_done = sem("last_half_done")
        mk_split = sem("mk_split")
        mem_v_rounded = sem("mem_v_rounded")
        mem_v_split = sem("mem_v_split")
        xq_hi_done = sem("xq_hi_done")
        xp_t_split = sem("xp_t_split")
        xs_done = sem("xs_done")
        x_maxed = sem("x_maxed")
        x_exp_done = sem("x_exp_done")
        x_scaled = sem("x_scaled")
        xp_turned = sem("xp_turned")
        xp_t_ready = sem("xp_t_ready")
        xo_done = sem("xo_done")
        xo_hi_done = sem("xo_hi_done")
        xo_lo_done = sem("xo_lo_done")
        tap2_done = sem("tap2_done")
        tap1_done = sem("tap1_done")
        conv_done = sem("conv_done")
        gelu_done = sem("gelu_done")
        gated = sem("gated")
        gate_hi_done = sem("gate_hi_done")
        gate_lo_done = sem("gate_lo_done")
        mask_step = sem("mask_step")
        count_ready = sem("count_ready")
        count_ln = sem("count_ln")
        dil_mask_made = sem("dil_mask_made")
        lam_summed = sem("lam_summed")
        eps_set = sem("eps_set")
        vec_step = sem("vec_step")
        act_step = sem("act_step")

        def fm_src(w, c0, n):
            return w[0].rearrange("(k p) c -> p k c", p=P)[:, :, bass.ds(c0, n)]

        def tm_src(w, k0, nk, c0, n):
            return w[0].rearrange("(k p) c -> p k c", p=P)[:, k0:k0 + nk, bass.ds(c0, n)]

        def fm_slot(t, s):
            return t[:, s, :].rearrange("p (k c) -> p k c", k=KT)

        def tm_slot(t, s, nk=4):
            return t[:, s, 0:nk * HALF].rearrange("p (k c) -> p k c", k=nk)

        doubled = [UNIT0["v"], UNIT0["v"] + 1]

        def loaded_value(u):
            return 16 * (u // 2 + 1 + sum(1 for d in doubled if d % 2 == u % 2 and d <= u))

        FQ, FK, FV, FF = 0, FOX_W, 2 * FOX_W, 3 * FOX_W
        DQ = FF + FOX
        DK, DV = DQ + DIFF_W, DQ + 2 * DIFF_W
        CQ = DQ + 3 * DIFF_W
        CK, CV = CQ + DIL_W, CQ + 2 * DIL_W

        block = ctx.enter_context(nc.Block())

        @block.sync
        def _(sp):
            def load(u, dst, src):
                if u >= 2:
                    sp.wait_ge(split_done, u - 1)
                if u - 2 in SHARED:
                    sp.wait_ge(vec_split, SHARED.index(u - 2) + 1)
                sp.dma_start(dst, src).then_inc(raw_loaded[u % 2], 16)

            def load_tm_halves(phase, w, c0):
                for h in range(2):
                    for k in range(2):
                        load(UNIT0[phase] + 2 * h + k, tm_slot(raw, k), tm_src(w, 4 * k, 4, c0 + HALF * h, HALF))

            sp.dma_start(x_tok[:, 0, :], x[0, 0:P, :]).then_inc(x_loaded[0], 16)
            for k in range(2):
                load(UNIT0["v"] + k, tm_slot(raw, k)[:, :, 0:FOX_W], tm_src(w_in, 4 * k, 4, FV, FOX_W))
                sp.dma_start(tm_slot(raw, k)[:, :, FOX_W:HALF],
                             tm_src(w_in, 4 * k, 4, DV, DIFF_W)).then_inc(raw_loaded[k], 16)
                for t in range(1, TT if k == 0 else 1):
                    sp.dma_start(x_tok[:, t, :], x[0, t * P:(t + 1) * P, :]).then_inc(x_loaded[t], 16)
            for k in range(2):
                load(UNIT0["v"] + 2 + k, tm_slot(raw, k), tm_src(w_in, 4 * k, 4, CV, HALF))
            for n, c in enumerate([FQ, FK, DQ, DK, CQ, CK, CQ + 256, CK + 256]):
                load(UNIT0["qk"] + n, fm_slot(raw, n % 2), fm_src(w_in, c, 256))
            load_tm_halves("mv", w_mkv, D)
            load_tm_halves("wo", w_o, 0)
            sp.wait_ge(scored, N_MAPS)
            sp.dma_start(side_gain[:, 0, :], ln1_g.to_broadcast([P, D])).then_inc(gains_loaded[0], 16)
            sp.dma_start(side_gain[:, 1, :], ln1_b.to_broadcast([P, D])).then_inc(gains_loaded[0], 16)
            load_tm_halves("mk", w_mkv, 0)
            for n in range(4):
                load(UNIT0["mq"] + n, fm_slot(raw, n % 2), fm_src(w_mq, 256 * n, 256))
            sp.wait_ge(ln_applied[0], TT)
            sp.dma_start(side_gain[:, 0, :], ln2_g.to_broadcast([P, D])).then_inc(gains_loaded[1], 16)
            sp.dma_start(side_gain[:, 1, :], ln2_b.to_broadcast([P, D])).then_inc(gains_loaded[1], 16)
            load_tm_halves("mo", w_mo, 0)
            u0 = UNIT0["up"]
            with sp.Fori(0, FT // 2) as t:
                for s in range(2):
                    sp.wait_ge(split_done, 2 * t + (u0 + s - 1))
                    sp.dma_start(fm_slot(raw, s), fm_src(w_up, 256 * t + s * D_FF, 256)).then_inc(raw_loaded[s], 16)
            u0 = UNIT0["down"]
            with sp.Fori(0, 2) as h:
                for n in range(6):
                    sp.wait_ge(split_done, 6 * h + (u0 + n - 1))
                    sp.dma_start(tm_slot(raw, n % 2, DOWN_KT[n]),
                                 tm_src(w_down, DOWN_K0[n], DOWN_KT[n], HALF * h, HALF)).then_inc(raw_loaded[n % 2], 16)
            sp.wait_ge(gate_lo_done, 2 + FT)
            sp.dma_start(side_gain[:, 0, :], ln3_g.to_broadcast([P, D])).then_inc(gains_loaded[2], 16)
            sp.dma_start(side_gain[:, 1, :], ln3_b.to_broadcast([P, D])).then_inc(gains_loaded[2], 16)
            def store(t, cols=slice(0, D)):
                sp.dma_start(out[0, t * P:(t + 1) * P, cols], x_tok[:, t, cols]).then_inc(stored, 16)

            sp.wait_ge(ln_applied[2], 1)
            store(0)
            for h in range(2):
                sp.wait_ge(last_half_done, h + 1)
                store(3, slice(HALF * h, HALF * (h + 1)))
            sp.wait_ge(ln_applied[2], 2)
            store(1)
            sp.wait_ge(third_done, 1)
            store(2)
            sp.wait_ge(stored, 16 * (TT + 1))

        @block.gpsimd
        def _(pool):
            pool.memset(ident[:, :], 0.0).then_inc(masks_zeroed, 1)
            pool.memset(causal[:, :], 0.0).then_inc(masks_zeroed, 1)
            pool.memset(prob_t[0:FOX, 0, :], 0.0).then_inc(masks_zeroed, 1)
            pool.wait_ge(masks_zeroed, 3)
            pool.affine_select(out=ident[:, :], in_=ident[:, :], compare_op=ALU.not_equal, fill=1.0, base=0,
                               pattern=[[-1, P]], channel_multiplier=1).then_inc(ident_made, 1)
            pool.iota(dist[:, :], [[-1, SEQ]], base=SEQ - P, channel_multiplier=1,
                      allow_small_or_imprecise_dtypes=True).then_inc(masks_made, 1)
            pool.affine_select(out=causal[:, :], in_=causal[:, :], compare_op=ALU.is_ge, fill=NEG, base=SEQ - P,
                               pattern=[[-1, SEQ]], channel_multiplier=1).then_inc(masks_made, 1)
            pool.affine_select(out=fsel, in_=fsel, compare_op=ALU.not_equal, fill=1.0, base=0,
                               pattern=[[-1, FOX], [0, P]], channel_multiplier=1).then_inc(masks_made, 1)
            pool.iota(prob_rows[:, 3, :].bitcast(I32), [[-1, SEQ]], base=SEQ - P,
                      channel_multiplier=1).then_inc(masks_made, 1)

            def split(u, s, free_chunks):
                c0 = VEC_PART if u in SHARED else 0
                pool.wait_ge(raw_loaded[s], loaded_value(u))
                if free_chunks is not None:
                    pool.wait_ge(dense_done, free_chunks)
                pool.tensor_scalar(w_hi[:, s, c0:], raw[:, s, c0:], 1.0, 0.0, ALU.mult, ALU.add).then_inc(hi_split, 1)
                pool.wait_ge(hi_split, u + 1)
                pool.tensor_tensor(w_lo[:, s, c0:], raw[:, s, c0:], w_hi[:, s, c0:].bitcast(F32),
                                   ALU.subtract).then_inc(split_done, 1)

            chunks_to = [0] * (N_UNITS + 1)
            for name, _, n, ch in PHASES:
                for j in range(n):
                    chunks_to[UNIT0[name] + j + 1] = chunks_to[UNIT0[name] + j] + ch

            def split_units(first, last):
                for u in range(first, last):
                    split(u, u % 2, chunks_to[u - 1] if u >= 2 else None)

            split_units(0, UNIT0["mv"] + 2)

            def make_bias(n):
                slot = side[:, n % 4, :]
                if n == 0:
                    pool.wait_ge(cols_ready, 2)
                    pool.wait_ge(lam_exp, 1)
                if n >= 4:
                    pool.wait_ge(scored, LAST_MAP_OF_ITEM[n - 4] + 1)
                if DIFF <= n < DIFF + FOX * TT:
                    h, i = (n - DIFF) // TT, (n - DIFF) % TT
                    w = (i + 1) * P
                    if n == DIFF:
                        pool.wait_ge(forget_q_ready, 1)
                        pool.wait_ge(forget_k_ready, FOX)
                    pool.tensor_scalar(slot[:, 0:w], causal[:, SEQ - w:SEQ], forget_q[:, i, h:h + 1], 1.0,
                                       ALU.add, ALU.mult).then_inc(bias_scaled, 1)
                    pool.wait_ge(bias_scaled, n + 1)
                    pool.tensor_tensor(slot[:, 0:w], slot[:, 0:w], scratch[:, h, 0:w],
                                       ALU.subtract).then_inc(bias_made, 1)
                    return
                if n < DIFF:
                    slope, mask = DIFF_SLOPES[n], causal
                    pool.wait_ge(masks_made, 4)
                else:
                    slope, mask = DIL_SLOPES[n - DIFF - FOX * TT], dil_mask
                    pool.wait_ge(dil_mask_made, 1)
                pool.tensor_scalar(slot, dist[:, :], -slope, 1.0, ALU.mult, ALU.mult).then_inc(bias_scaled, 1)
                pool.wait_ge(bias_scaled, n + 1)
                pool.tensor_tensor(slot, slot, mask[:, :], ALU.add).then_inc(bias_made, 1)

            for n in range(N_ITEMS):
                make_bias(n)
                if n in (DIFF + FOX * TT, DIFF + FOX * TT + 1):
                    u = UNIT0["mv"] + 2 + n - DIFF - FOX * TT
                    split_units(u, u + 1)
            split_units(UNIT0["wo"], UNIT0["up"])
            rounded = pool.alloc_register("rounded")
            u0 = UNIT0["up"]
            pool.reg_mov(rounded, u0)
            with pool.Fori(0, FT // 2) as t:
                for s in range(2):
                    u = u0 + s
                    pool.wait_ge(raw_loaded[s], 16 * t + loaded_value(u))
                    pool.wait_ge(dense_done, 4 * t + (chunks_to[u0] + 2 * (s - 1)))
                    pool.reg_add(rounded, rounded, 1)
                    pool.tensor_scalar(w_hi[:, s, :], raw[:, s, :], 1.0, 0.0, ALU.mult, ALU.add).then_inc(hi_split, 1)
                    pool.wait_ge(hi_split, rounded)
                    pool.tensor_tensor(w_lo[:, s, :], raw[:, s, :], w_hi[:, s, :].bitcast(F32),
                                       ALU.subtract).then_inc(split_done, 1)
            u0 = UNIT0["down"]
            with pool.Fori(0, 2) as h:
                for n in range(6):
                    u, s, w = u0 + n, n % 2, DOWN_KT[n] * HALF
                    pool.wait_ge(raw_loaded[s], 48 * h + loaded_value(u))
                    pool.wait_ge(dense_done, chunks_to[u - 1])
                    pool.wait_ge(dense_done, 24 * h + (chunks_to[u0] + 4 * (n - 1)))
                    pool.reg_add(rounded, rounded, 1)
                    pool.tensor_scalar(w_hi[:, s, 0:w], raw[:, s, 0:w], 1.0, 0.0, ALU.mult,
                                       ALU.add).then_inc(hi_split, 1)
                    pool.wait_ge(hi_split, rounded)
                    pool.tensor_tensor(w_lo[:, s, 0:w], raw[:, s, 0:w], w_hi[:, s, 0:w].bitcast(F32),
                                       ALU.subtract).then_inc(split_done, 1)

            pool.wait_ge(gains_loaded[2], 32)
            for t in range(2):
                pool.wait_ge(last_z_ready, t + 1)
                pool.tensor_tensor(x_tok[:, t, :], x_tok[:, t, :], side_gain[:, 0, :], ALU.mult)\
                    .then_inc(last_gained, 1)
                pool.wait_ge(last_gained, t + 1)
                pool.tensor_tensor(x_tok[:, t, :], x_tok[:, t, :], side_gain[:, 1, :], ALU.add)\
                    .then_inc(ln_applied[2], 1)

        @block.tensor
        def _(pe):
            def fm_unit(s, done_value, bank, bank_free, operand_ready=None):
                pe.wait_ge(split_done, done_value)
                for q in range(2):
                    bank_free(q)
                    for k in range(KT):
                        if operand_ready and q == 0:
                            operand_ready(k)
                        for n, (w, a) in enumerate([(w_hi, act_hi), (w_hi, act_lo), (w_lo, act_hi)]):
                            mm = pe.matmul(ps[:, bank + q, :], fm_slot(w, s)[:, k, q * P:(q + 1) * P],
                                           a[:, k, :], start=(k == 0 and n == 0),
                                           stop=(k == KT - 1 and n == 2))
                    mm.then_inc(dense_done, 1)

            def tm_unit(s, done_value, a_hi, a_lo, k0, nk, first, last, bank_free, tiles, bank=0):
                pe.wait_ge(split_done, done_value)
                for t in range(tiles):
                    if first:
                        bank_free(t)
                    for k in range(nk):
                        for n, (w, a) in enumerate([(w_hi, a_hi), (w_hi, a_lo), (w_lo, a_hi)]):
                            out_bank = ps[:, bass.ds(bank + t, 1), :].rearrange("p a b -> p (a b)")
                            mm = pe.matmul(out_bank, a[:, k0 + k, t * P:(t + 1) * P], tm_slot(w, s, nk)[:, k, :],
                                           start=(first and k == 0 and n == 0),
                                           stop=(last and k == nk - 1 and n == 2))
                    mm.then_inc(dense_done, 1)

            def tm_phase(phase, evac, a_hi=act_hi, a_lo=act_lo, tiles=TT, before_last_tile=lambda: None,
                         before_unit=lambda h, k: None):
                pe.sem_inc(evac, tiles)
                with pe.Fori(0, 2) as h:
                    for k in range(2):
                        def bank_free(t):
                            if t == tiles - 1:
                                before_last_tile()
                            pe.wait_ge(evac, tiles * h + (t + 1))

                        before_unit(h, k)
                        tm_unit(k, 2 * h + (UNIT0[phase] + k + 1), a_hi, a_lo, 4 * k, 4, k == 0, k == 1,
                                bank_free, tiles)

            def fm_phase(phase, evac, pairs, operand_ready=None):
                pe.sem_inc(evac, 4)

                def pair(t, ready=None):
                    for s in range(2):
                        fm_unit(s, 2 * t + (UNIT0[phase] + s + 1), 2 * s,
                                lambda q, s=s: pe.wait_ge(evac, 4 * t + (2 * s + q + 1)),
                                ready if s == 0 else None)

                if operand_ready:
                    pair(0, operand_ready)
                with pe.Fori(1 if operand_ready else 0, pairs) as t:
                    pair(t)

            def turn_x(t):
                pe.wait_ge(x_loaded[t], 16)
                for n in (2 * t, 2 * t + 1):
                    if n >= 4:
                        pe.wait_ge(x_lo_done, n - 3)
                    for k in range(4):
                        kt = 4 * (n % 2) + k
                        mm = pe.transpose(ps[:, 4 + n % 4, k * P:(k + 1) * P], x_tok[:, t, kt * P:(kt + 1) * P],
                                          ident[:, :])
                    mm.then_inc(x_turned, 1)

            pe.wait_ge(ident_made, 1)
            turn_x(0)
            pe.wait_ge(vec_split, 1)

            def x_tile_ready(t):
                if t + 1 < TT:
                    turn_x(t + 1)
                pe.wait_ge(x_lo_done, 2 * t + 1)

            tm_unit(0, 1, act_hi, act_lo, 0, 4, True, False, x_tile_ready, TT)
            pe.wait_ge(x_lo_done, 2 * TT)
            pe.wait_ge(gate_chain, 2)
            for k in range(KT):
                for n, (w, a) in enumerate([(wff_hi, act_hi), (wff_hi, act_lo), (wff_lo, act_hi)]):
                    mm = pe.matmul(ps[0:FOX, 4, :], w[:, k, :], a[:, k, :], start=(k == 0 and n == 0),
                                   stop=(k == KT - 1 and n == 2))
            mm.then_inc(ff_summed, 1)
            pe.wait_ge(vec_split, 2)
            tm_unit(1, 2, act_hi, act_lo, 4, 4, False, True, None, TT)
            for k in range(2):
                tm_unit(k, 3 + k, act_hi, act_lo, 4 * k, 4, k == 0, k == 1, lambda t: pe.wait_ge(v_evac, t + 1), TT)
            pe.wait_ge(v_evac, 2 * TT)
            fm_phase("qk", qk_evac, 4)
            pe.wait_ge(gate_chain, 6)
            for i in range(TT):
                mm = pe.transpose(ps[:, 5, i * FOX:(i + 1) * FOX], fg[:, 2, i * P:(i + 1) * P],
                                  ident[0:FOX, 0:FOX])
            mm.then_inc(forget_turned, 1)
            pe.wait_ge(rows_loaded, 16 * 8)
            for r in range(8):
                n = 2 * FT if r < 4 else KT
                mm = pe.transpose(ps[:, 6, r * 2 * FT:r * 2 * FT + n], side_rows[0:n, r, :], ident[0:n, 0:n])
            mm.then_inc(rows_turned, 1)
            for n in range(2 * MT):
                t, g = n // 2, n % 2
                if g == 0:
                    pe.wait_ge(mem_loaded[t], 16)
                if n < 2:
                    pe.wait_ge(forget_q_ready, 1)
                    pe.wait_ge(cols_ready, 2)
                for k in range(4):
                    mm = pe.transpose(ps[:, 4 + n, k * P:(k + 1) * P],
                                      mem_tok[:, t, (4 * g + k) * P:(4 * g + k + 1) * P], ident[:, :])
                mm.then_inc(mem_turned, 1)
            pe.wait_ge(masks_made, 3)
            for h in range(FOX):
                pe.wait_ge(mem_lo_done, 2 * MT)
                pe.matmul(ps[:, 4 + h, :], fsel[:, h, :], fg[:, 2, :], start=True, stop=True).then_inc(forget_spread, 1)

            pe.wait_ge(qk_evac, 4 + 16)

            def scores(s):
                hp, i = STEPS[s]
                for j, m in enumerate(maps_of(s)):
                    if m < 2:
                        pe.wait_ge(forget_k_ready, m + 1)
                    if m >= len(S_BANKS):
                        pe.wait_ge(scored, m - len(S_BANKS) + 1)
                    tq, tk, r, d = qk_place(hp, j)
                    pe.matmul(ps[:, S_BANKS[m % len(S_BANKS)], 0:(i + 1) * P], qk_t[r:r + d, tq, i * P:(i + 1) * P],
                              qk_t[r:r + d, tk, 0:(i + 1) * P], start=True, stop=True).then_inc(qk_done, 1)

            def turn_bank_free(turn):
                last = turn - 2
                if last in STEP_OF_TURN:
                    pe.wait_ge(prob_t_ready, STEP_OF_TURN[last] + 1)
                elif last in PAIR_OF_TURN:
                    pe.wait_ge(rms_scaled, 2 * PAIR_OF_TURN[last] + 1)

            def turn_probs(s):
                hp, i = STEPS[s]
                turn = TURN_OF_STEP[s]
                turn_bank_free(turn)
                if turn < 2:
                    pe.wait_ge(forget_k_ready, turn + 3)
                pe.wait_ge(normed, s + 1)
                c, _ = prob_place(maps_of(s)[0])
                for b in range(i + 1):
                    mm = pe.transpose(ps[:, T_BANKS[turn % 2], b * P:(b + 1) * P],
                                      prob[:, c + b * P:c + (b + 1) * P], ident[:, :])
                mm.then_inc(turned, 1)

            def weigh_values(s):
                hp, i = STEPS[s]
                head = HEAD_ORDER[hp]
                pe.wait_ge(prob_t_ready, s + 1)
                if i == 0 and hp % 2 == 0 and hp >= 4:
                    pe.wait_ge(o_lo_done, hp // 2 - 1)
                r = (hp % 2) * HD
                for b in range(i + 1):
                    mm = pe.matmul(ps[r:r + HD, O_BANKS[hp // 2 % 2], i * P:(i + 1) * P],
                                   v_tok[:, b, head * HD:(head + 1) * HD], prob_t[:, s % 2, b * P:(b + 1) * P],
                                   start=(b == 0), stop=(b == i))
                mm.then_inc(pv_done, 1)

            def sum_squares(p):
                turn = TURN_OF_PAIR[p]
                turn_bank_free(turn)
                pe.wait_ge(ones_made, 3)
                pe.wait_ge(squared, p + 1)
                pe.matmul(ps[:, T_BANKS[turn % 2], :], head_ones[:, :], rms_t(p), start=True,
                          stop=True).then_inc(rms_summed, 1)

            def fill(k):
                for n, first in enumerate(FILL_STARTS):
                    if not first <= k < first + FILL_STEPS:
                        continue
                    h, t = n // MT, n % MT
                    if k == first:
                        pe.wait_ge(split_done, UNIT0["mv"] + 2 * h + 2)
                        if n >= 1:
                            pe.wait_ge(mv_evac, n)
                    for item in range(FILL * (k - first), FILL * (k - first + 1)):
                        kt, (w, a) = item // 3, [(w_hi, mem_hi), (w_hi, mem_lo), (w_lo, mem_hi)][item % 3]
                        mm = pe.matmul(ps[:, FILL_BANK, :], a[:, kt, t * P:(t + 1) * P],
                                       tm_slot(w, kt // 4)[:, kt % 4, :], start=(item == 0), stop=(item == 3 * KT - 1))
                    if k == first + FILL_STEPS - 1:
                        mm.then_inc(mv_half, 1) if t == 0 else mm.then_inc(dense_done, 2 * CHUNKS["mv"])

            for s in range(AHEAD + 1):
                scores(s)
            for k in range(N_STEPS + 1):
                if k + AHEAD + 1 < N_STEPS:
                    scores(k + AHEAD + 1)
                fill(k)
                if k < N_STEPS:
                    turn_probs(k)
                if k >= 1:
                    weigh_values(k - 1)
                if k >= PAIR_LAG and (k - PAIR_LAG) % 8 == 0 and (k - PAIR_LAG) // 8 in TURN_OF_PAIR:
                    sum_squares((k - PAIR_LAG) // 8)

            def turn_z(n, k):
                if k >= 4:
                    pe.wait_ge([y_by_act, y_by_vec][k % 2][n], k // 2 - 1)
                for t in range(TT):
                    mm = pe.transpose(ps[:, 4 + k % 4, t * P:(t + 1) * P], x_tok[:, t, k * P:(k + 1) * P],
                                      ident[:, :])
                mm.then_inc(z_turned[n], 1)

            def turn_first_z(n):
                for t in range(TT):
                    pe.wait_ge(z_ready[n], t + 1)
                    for k in range(4):
                        mm = pe.transpose(ps[:, 4 + k, t * P:(t + 1) * P], x_tok[:, t, k * P:(k + 1) * P],
                                          ident[:, :])
                        if t == TT - 1:
                            mm.then_inc(z_turned[n], 1)

            def normed_ready(n, k):
                if 1 <= k < KT - 3:
                    turn_z(n, k + 3)
                pe.wait_ge(z_lo_done[n], k + 1)

            pe.wait_ge(o_lo_done, HEADS // 2 - 1)
            tm_phase("wo", res_done[0], before_last_tile=lambda: pe.wait_ge(o_lo_done, HEADS // 2))
            pe.wait_ge(res_done[0], 4 + 8)
            tm_phase("mk", mk_evac, mem_hi, mem_lo, MT,
                     before_unit=lambda h, k: pe.wait_ge(vec_split, h * (k + 1) + 2))
            pe.wait_ge(mk_evac, MT + 4)
            turn_first_z(0)

            def query_operand(k):
                normed_ready(0, k)
                if k < KT - 1:
                    return
                for n in range(4):
                    for f in range(2):
                        for m in range(MT):
                            c = (2 * n + f) * P
                            mm = pe.transpose(ps[:, 4 + n, (2 * f + m) * P:(2 * f + m + 1) * P],
                                              mem_k[:, m, c:c + P], ident[:, :])
                    mm.then_inc(mk_turned, 1)

            fm_phase("mq", mq_evac, 2, query_operand)

            def x_scores(c):
                h, i = c // TT, c % TT
                if c == 0:
                    pe.wait_ge(mk_split, 4)
                if i == 0:
                    pe.wait_ge(mq_evac, 4 + 2 * (h + 1))
                if c == 2:
                    pe.wait_ge(mq_evac, 4 + KT)
                if c >= 4:
                    pe.wait_ge(x_exp_done, c - 3)
                for f in range(2):
                    for n, (q, k) in enumerate([(xq_hi, mem_kt_hi), (xq_hi, mem_kt_lo), (xq_lo, mem_kt_hi)]):
                        mm = pe.matmul(ps[:, X_S_BANKS[c % 4], 0:MEM], q[:, 2 * h + f, i * P:(i + 1) * P],
                                       k[:, 2 * h + f, :], start=(f == 0 and n == 0), stop=(f == 1 and n == 2))
                mm.then_inc(xs_done, 1)

            def x_turn(c):
                if c % 2 == 0 and c >= 4:
                    pe.wait_ge(xp_t_split, c // 2 - 1)
                pe.wait_ge(x_scaled, c + 1)
                for m in range(MT):
                    mm = pe.transpose(ps[:, 6 + (c // 2) % 2, ((c % 2) * MT + m) * P:((c % 2) * MT + m + 1) * P],
                                      xp[:, c % 4, m * P:(m + 1) * P], ident[:, :])
                mm.then_inc(xp_turned, 1)

            def x_weigh(h):
                pe.wait_ge(xp_t_split, 2 * h + 2)
                pe.wait_ge(mem_v_split, 1)
                for f in range(2):
                    if h == MEM_HEADS - 1:
                        pe.wait_ge(x_exp_done, N_X)
                    elif h >= 1:
                        pe.wait_ge(xo_lo_done, 2 * (h - 1) + f + 1)
                    for m in range(MT):
                        c = (2 * h + f) * P
                        for n, (v, p) in enumerate([(mem_v_hi, xp_t_hi), (mem_v_hi, xp_t_lo), (mem_v_lo, xp_t_hi)]):
                            mm = pe.matmul(ps[:, X_O_BANK[h] + f, :], v[:, m, c:c + P], p[:, h % 2, m, :],
                                           start=(m == 0 and n == 0), stop=(m == MT - 1 and n == 2))
                    mm.then_inc(xo_done, 1)

            N_X = MEM_HEADS * TT
            for c in range(X_AHEAD + 1):
                x_scores(c)
            for c in range(N_X + 2):
                if c + X_AHEAD + 1 < N_X:
                    x_scores(c + X_AHEAD + 1)
                if c < N_X:
                    x_turn(c)
                if c >= TT + 1 and (c - TT - 1) % TT == 0:
                    x_weigh((c - TT - 1) // TT)
            pe.wait_ge(xo_lo_done, KT - 2)
            tm_phase("mo", res_done[1],
                     before_unit=lambda h, k: pe.wait_ge(xo_lo_done, KT) if k == 1 else None)
            pe.wait_ge(res_done[1], 4 + 8)
            turn_first_z(1)

            fm_phase("up", conv_done, FT // 2, lambda k: normed_ready(1, k))
            with pe.Fori(0, 2) as h:
                for n in range(6):
                    pe.wait_ge(gate_lo_done, 2 + DOWN_K0[n] + DOWN_KT[n])
                    tm_unit(n % 2, 6 * h + (UNIT0["down"] + n + 1), gate_hi, gate_lo, DOWN_K0[n], DOWN_KT[n],
                            n == 0, n == 5, lambda t: pe.wait_ge(conv_done, 2 * FT * h + (t + 1)), TT,
                            4 - 4 * h)

        @block.scalar
        def _(act):
            steps = [0]

            def chain(ins):
                steps[0] += 1
                ins.then_inc(act_step, 1)
                act.wait_ge(act_step, steps[0])

            act.dma_start(wff[:, :, :], fm_src(w_in, FF, FOX)).then_inc(gate_w_loaded, 16)
            act.dma_start(bf_col[:, :], b_f.rearrange("a h -> h a")).then_inc(gate_w_loaded, 16)
            act.preload_act_table_set("natural_log_exp_and_others")

            for n in range(2 * TT):
                t, g = n // 2, n % 2
                act.wait_ge(x_turned, n + 1)
                act.activation(act_hi[:, 4 * g:4 * g + 4, t * P:(t + 1) * P],
                               ps[:, 4 + n % 4, :].rearrange("p (k t) -> p k t", k=4), ACT.Copy).then_inc(x_hi_done, 1)
            for r in range(3):
                act.dma_start(side_rows[0:2 * FT, r, :],
                              conv_w[0, r].rearrange("a (j p) -> (a j) p", p=P)).then_inc(rows_loaded, 16)
            act.dma_start(side_rows[0:2 * FT, 3, :], conv_b[0].rearrange("(j p) -> j p", p=P)).then_inc(rows_loaded, 16)
            for r, v in enumerate([ln1_g, ln1_b, ln2_g, ln2_b]):
                act.dma_start(side_rows[0:KT, 4 + r, :], v[0].rearrange("(j p) -> j p", p=P)).then_inc(rows_loaded, 16)
            for r, v in enumerate([lq1, lk1, lq2, lk2]):
                act.dma_start(lam_in[:, r, :], v.to_broadcast([P, HD // 2])).then_inc(lam_loaded, 16)
            for h in range(2):
                act.dma_start(diff_gain[h * HD:(h + 1) * HD, :], diff_g.rearrange("a d -> d a")).then_inc(lam_loaded, 16)
            for t in range(MT):
                act.dma_start(mem_tok[:, t, :], mem[0, t * P:(t + 1) * P, :]).then_inc(mem_loaded[t], 16)
            act.wait_ge(count_ready, 1)
            act.activation(dil_mask[:, :], prob_rows[:, 0, :], ACT.Ln).then_inc(count_ln, 1)
            act.wait_ge(lam_summed, 2)
            act.activation(lam_s[:, 2:4], lam_s[:, 0:2], ACT.Exp).then_inc(lam_exp, 1)
            act.wait_ge(gate_chain, 4)
            act.activation(fg[:, 2, :], fg[:, 1, :], ACT.Exp, scale=-1.0).then_inc(gate_exp, 1)
            act.wait_ge(gate_exp, 1)
            act.activation(fg[:, 1, :], fg[:, 2, :], ACT.Ln, bias=1.0).then_inc(gate_exp, 1)
            for n in range(2 * TT):
                h, t = n // TT, n % TT
                act.wait_ge(dense_done, chunks_through("v", 2 * h + 1) + t + 1)
                act.activation(v_tok[:, t, HALF * h:HALF * (h + 1)], ps[:, t, :], ACT.Copy).then_inc(v_evac, 1)
            for n in range(16):
                act.wait_ge(dense_done, CHUNK0["qk"] + n + 1)
                scale = 1.0
                if n % 4 < 2:
                    scale = float(np.float32((HD // 2) ** -0.5)) if 4 <= n < 8 else HD ** -0.5
                act.activation(qk_t[:, n, :], ps[:, n % 4, :], ACT.Copy, scale=scale).then_inc(qk_evac, 1)
            act.wait_ge(rows_turned, 1)
            act.activation(conv_cols[:, :, :], ps[:, 6, 0:8 * FT].rearrange("p (r f) -> p r f", r=4), ACT.Copy)\
               .then_inc(cols_ready, 1)
            act.activation(ln_cols[:, :, :], ps[:, 6, 8 * FT:16 * FT].rearrange("p (r f) -> p r f", r=4)[:, :, 0:KT],
                           ACT.Copy).then_inc(cols_ready, 1)
            for n in range(2 * MT):
                t, g = n // 2, n % 2
                act.wait_ge(mem_turned, n + 1)
                act.activation(mem_hi[:, 4 * g:4 * g + 4, t * P:(t + 1) * P],
                               ps[:, 4 + n, :].rearrange("p (k t) -> p k t", k=4), ACT.Copy).then_inc(mem_hi_done, 1)
            for h in range(FOX):
                act.wait_ge(forget_spread, h + 1)
                act.activation(scratch[:, h, :], ps[:, 4 + h, :], ACT.Copy).then_inc(forget_k_ready, 1)

            def exps(s):
                hp, i = STEPS[s]
                for j, m in enumerate(maps_of(s)):
                    act.wait_ge(scored, m + 1)
                    c, _ = prob_place(m)
                    row = prob[:, c:c + (i + 1) * P]
                    act.activation(row, row, ACT.Exp, bias=neg_max[:, m:m + 1], scale=-1.0,
                                   accum_out=den[:, j, s:s + 1]).then_inc(exp_done, 1)

            def keep_probs(s):
                hp, i = STEPS[s]
                turn = TURN_OF_STEP[s]
                act.wait_ge(turned, s + 1)
                if s >= 2:
                    act.wait_ge(pv_done, s - 1)
                w = (i + 1) * P
                act.activation(prob_t[:, s % 2, 0:w], ps[:, T_BANKS[turn % 2], 0:w], ACT.Copy).then_inc(prob_t_ready, 1)

            def square(p):
                act.wait_ge(pv_done, 8 * (p + 1))
                act.activation(rms_t(p), ps[:, O_BANKS[p % 2], :], ACT.Square).then_inc(squared, 1)

            def find_rms(p):
                act.wait_ge(rms_summed, p + 1)
                act.wait_ge(eps_set, 1)
                act.activation(rms_t(p), ps[:, T_BANKS[TURN_OF_PAIR[p] % 2], :], ACT.Ln, scale=1.0 / HD,
                               bias=eps[:, :]).then_inc(rms_scaled, 1)
                act.wait_ge(rms_scaled, 2 * p + 1)
                act.activation(rms_t(p), rms_t(p), ACT.Exp, scale=-0.5).then_inc(rms_scaled, 1)

            def output_high(p):
                if is_diff(2 * p):
                    act.wait_ge(o_rmsed, p + 1)
                    src = rms_t(p)
                else:
                    act.wait_ge(pv_done, 8 * (p + 1))
                    src = ps[:, O_BANKS[p % 2], :]
                act.activation(act_hi[:, HEAD_ORDER[2 * p] // 2, :], src, ACT.Copy).then_inc(o_hi_done, 1)

            for s in range(AHEAD):
                exps(s)
            for k in range(N_STEPS + 1):
                if k + AHEAD < N_STEPS:
                    exps(k + AHEAD)
                if k < N_STEPS:
                    keep_probs(k)
                if k - FILL_STEPS + 1 in FILL_STARTS:
                    n = FILL_STARTS.index(k - FILL_STEPS + 1)
                    h, t = n // MT, n % MT
                    if t == 0:
                        act.wait_ge(mv_half, h + 1)
                    else:
                        act.wait_ge(dense_done, chunks_through("mv", 2 * h + 2))
                    act.activation(mem_v[:, t, HALF * h:HALF * (h + 1)], ps[:, FILL_BANK, :], ACT.Copy)\
                       .then_inc(mv_evac, 1)
                if k >= 8 and k % 8 == 0:
                    if is_diff(2 * (k // 8 - 1)):
                        square(k // 8 - 1)
                    else:
                        output_high(k // 8 - 1)
                if k % 8 == PAIR_LAG % 8 and (k - PAIR_LAG) // 8 in TURN_OF_PAIR:
                    find_rms((k - PAIR_LAG) // 8)
                if k % 8 == (PAIR_LAG + 1) % 8 and (k - PAIR_LAG) // 8 in TURN_OF_PAIR:
                    output_high((k - PAIR_LAG) // 8)

            def ln_rstd(n):
                for t in range(TT):
                    act.wait_ge(var_ready[n], t + 1)
                    chain(act.activation(ln_var[:, t:t + 1], mean_var[:, t, 1:2], ACT.Ln, bias=eps[:, :]))
                    act.activation(rstd[:, t:t + 1], ln_var[:, t:t + 1], ACT.Exp, scale=-0.5).then_inc(rstd_ready[n], 1)

            def ln_high(n):
                def apply(k):
                    act.wait_ge(z_turned[n], k + 1)
                    if k >= 4:
                        act.wait_ge(z_lo_done[n], k - 3)
                    act.activation(scratch[:, k % 4, :], ps[:, 4 + k % 4, :], ACT.Identity,
                                   scale=ln_cols[:, 2 * n, k:k + 1], bias=ln_cols[:, 2 * n + 1, k:k + 1])\
                       .then_inc(y_by_act[n], 1)

                apply(0)
                for k in range(KT):
                    if k % 2 == 1 and k + 1 < KT:
                        apply(k + 1)
                    act.wait_ge([y_by_act, y_by_vec][k % 2][n], k // 2 + 1)
                    act.activation(act_hi[:, k, :], scratch[:, k % 4, :], ACT.Copy).then_inc(z_hi_done[n], 1)

            ln_rstd(0)
            for n in range(2 * MT):
                h, t = n // MT, n % MT
                act.wait_ge(dense_done, chunks_through("mk", 2 * h + 1) + t + 1)
                act.activation(mem_k[:, t, HALF * h:HALF * (h + 1)], ps[:, t, :], ACT.Copy).then_inc(mk_evac, 1)
            ln_high(0)
            for n in range(4):
                act.wait_ge(mk_turned, n + 1)
                act.activation(mem_kt_hi[:, 2 * n:2 * n + 2, :], ps[:, 4 + n, :].rearrange("p (f m) -> p f m", f=2),
                               ACT.Copy).then_inc(mk_ready, 1)
            act.wait_ge(mk_turned, 4)
            act.activation(mem_v_hi, mem_v[:, :, :], ACT.Copy).then_inc(mem_v_rounded, 1)
            for n in range(KT):
                act.wait_ge(dense_done, CHUNK0["mq"] + n + 1)
                act.activation(xq_hi[:, n, :], ps[:, n % 4, :], ACT.Copy, scale=X_SCALE).then_inc(xq_hi_done, 1)

            N_X = MEM_HEADS * TT

            def x_exp(c):
                act.wait_ge(x_maxed, c + 1)
                if c >= 4:
                    act.wait_ge(xp_turned, c - 3)
                act.activation(xp[:, c % 4, :], ps[:, X_S_BANKS[c % 4], 0:MEM], ACT.Exp, bias=x_neg_max[:, c:c + 1],
                               accum_out=x_den[:, c:c + 1]).then_inc(x_exp_done, 1)

            def x_keep(pair):
                h, i = pair // 2, 2 * (pair % 2)
                act.wait_ge(xp_turned, 2 * pair + 2)
                if h >= 2:
                    act.wait_ge(xo_done, 2 * (h - 1))
                for t in range(2):
                    ins = act.activation(xp_t_hi[:, h % 2, :, (i + t) * P:(i + t + 1) * P],
                                         ps[:, 6 + pair % 2, t * MT * P:(t + 1) * MT * P]
                                         .rearrange("p (m q) -> p m q", m=MT), ACT.Copy)
                ins.then_inc(xp_t_ready, 1)

            def xo_high(h):
                for f in range(2):
                    act.wait_ge(xo_done, 2 * h + f + 1)
                    act.activation(act_hi[:, 2 * h + f, :], ps[:, X_O_BANK[h] + f, :], ACT.Copy).then_inc(xo_hi_done, 1)

            for c in range(X_AHEAD):
                x_exp(c)
            for c in range(N_X + X_O_LAG + 1):
                if c + X_AHEAD < N_X:
                    x_exp(c + X_AHEAD)
                if c < N_X and c % 2 == 1:
                    x_keep(c // 2)
                if c >= TT + X_O_LAG and (c - TT - X_O_LAG) % TT == 0:
                    xo_high((c - TT - X_O_LAG) // TT)
            ln_rstd(1)
            ln_high(1)

            act.wait_ge(z_lo_done[1], KT)
            act.sem_inc(gelu_done, 2)
            act.sem_inc(gated, 2)
            with act.Fori(0, FT // 2) as t:
                def tap2(q, tile0):
                    act.wait_ge(dense_done, 4 * t + (CHUNK0["up"] + q + 1))
                    if q < 2:
                        act.wait_ge(gelu_done, 2 * t + (q + 1))
                    else:
                        act.wait_ge(gated, 2 * t + (q - 1))
                    act.wait_ge(cols_ready, 2)
                    act.activation(scratch[:, q, :], ps[:, q, :], ACT.Identity,
                                   scale=conv_cols[:, 2, bass.ds(2 * t + tile0, 1)],
                                   bias=conv_cols[:, 3, bass.ds(2 * t + tile0, 1)]).then_inc(tap2_done, 1)

                tap2(0, 0)
                tap2(1, 1)
                for q in range(2):
                    act.wait_ge(conv_done, 4 * t + (4 + q + 1))
                    act.wait_ge(gated, 2 * t + (q + 1))
                    act.activation(side[:, q, :], scratch[:, q, :], ACT.Gelu_apprx_tanh).then_inc(gelu_done, 1)
                tap2(2, FT)
                tap2(3, FT + 1)
                for q in range(2):
                    act.wait_ge(gated, 2 * t + (2 + q + 1))
                    act.wait_ge(cols_ready, 2)
                    act.activation(gate_hi[:, bass.ds(2 * t + q, 1), :].rearrange("p a b -> p (a b)"),
                                   side[:, 2 + q, :], ACT.Copy).then_inc(gate_hi_done, 1)
            act.preload_act_table_set("natural_log_exp_and_others")
            for t in range(TT):
                act.wait_ge(var_ready[2], t + 1)
                chain(act.activation(ln_var[:, t:t + 1], mean_var[:, t, 1:2], ACT.Ln, bias=eps[:, :]))
                rstd_made = act.activation(rstd[:, t:t + 1], ln_var[:, t:t + 1], ACT.Exp, scale=-0.5)
                if t == TT - 1:
                    rstd_made.then_inc(rstd_ready[2], 1)
                    break
                chain(rstd_made)
                act.wait_ge(neg_mean_ready, t + 1)
                chain(act.activation(ln_shift[:, t:t + 1], neg_mean[:, t:t + 1], ACT.Copy, scale=rstd[:, t:t + 1]))
                act.activation(x_tok[:, t, :], x_tok[:, t, :], ACT.Identity, scale=rstd[:, t:t + 1],
                               bias=ln_shift[:, t:t + 1]).then_inc(last_z_ready, 1)

        @block.vector
        def _(vec):
            steps = [0]

            def chain(ins):
                steps[0] += 1
                ins.then_inc(vec_step, 1)
                vec.wait_ge(vec_step, steps[0])

            def sub_hi(dst, src, hi):
                return vec.tensor_tensor(dst, src, hi.bitcast(F32), ALU.subtract)

            vec.memset(head_ones[:, :], 0.0).then_inc(ones_made, 1)
            vec.wait_ge(ones_made, 1)
            for h in range(2):
                vec.memset(head_ones[h * HD:(h + 1) * HD, h * HD:(h + 1) * HD], 1.0).then_inc(ones_made, 1)
            vec.wait_ge(gate_w_loaded, 32)
            vec.tensor_copy(wff_hi[:, :, :], wff[:, :, :]).then_inc(gate_chain, 1)
            vec.wait_ge(gate_chain, 1)
            sub_hi(wff_lo[:, :, :], wff[:, :, :], wff_hi[:, :, :]).then_inc(gate_chain, 1)
            def split_part(n, free_chunks=None):
                u, cols = SHARED[n], slice(0, VEC_PART)
                hi, lo, src = w_hi[:, u % 2, cols], w_lo[:, u % 2, cols], raw[:, u % 2, cols]
                vec.wait_ge(raw_loaded[u % 2], loaded_value(u))
                if free_chunks is not None:
                    vec.wait_ge(dense_done, free_chunks)
                vec.tensor_copy(hi, src).then_inc(vec_rounded, 1)
                vec.wait_ge(vec_rounded, n + 1)
                sub_hi(lo, src, hi).then_inc(vec_split, 1)

            for n in range(2 * TT):
                t, g = n // 2, n % 2
                vec.wait_ge(x_hi_done, n + 1)
                sub_hi(act_lo[:, 4 * g:4 * g + 4, t * P:(t + 1) * P],
                       ps[:, 4 + n % 4, :].rearrange("p (k t) -> p k t", k=4),
                       act_hi[:, 4 * g:4 * g + 4, t * P:(t + 1) * P]).then_inc(x_lo_done, 1)
                if n in (1, 3):
                    split_part(n // 2)
            masks = [0]

            def mask_chain(ins):
                masks[0] += 1
                ins.then_inc(mask_step, 1)
                vec.wait_ge(mask_step, masks[0])

            count, m4, m16 = prob_rows[:, 0, :], prob_rows[:, 1, :], prob_rows[:, 2, :]
            dist_i = prob_rows[:, 3, :].bitcast(I32)
            vec.wait_ge(masks_made, 4)
            mask_chain(vec.tensor_scalar(m4.bitcast(I32), dist_i, 3, None, ALU.bitwise_and))
            mask_chain(vec.tensor_scalar(m16.bitcast(I32), dist_i, 15, None, ALU.bitwise_and))
            mask_chain(vec.tensor_scalar(dil_mask[:, :], m4.bitcast(I32), 0.0, None, ALU.is_equal))
            mask_chain(vec.scalar_tensor_tensor(count, dist[:, :], float(P), dil_mask[:, :], ALU.is_le, ALU.add))
            mask_chain(vec.scalar_tensor_tensor(m4, m16.bitcast(I32), 0.0, count, ALU.is_equal, ALU.add))
            vec.tensor_scalar(count, m4, 1.0, None, ALU.max).then_inc(count_ready, 1)
            mask_chain(vec.tensor_scalar(m16, m4, 0.0, NEG, ALU.is_equal, ALU.mult))
            vec.wait_ge(count_ln, 1)
            mask_chain(vec.tensor_tensor(dil_mask[:, :], dil_mask[:, :], causal[:, :], ALU.add))
            vec.tensor_tensor(dil_mask[:, :], dil_mask[:, :], m16, ALU.add).then_inc(dil_mask_made, 1)
            vec.wait_ge(lam_loaded, 16 * 6)
            for n in range(2):
                vec.tensor_tensor_reduce(lam_in[:, 2 * n, :], lam_in[:, 2 * n, :], lam_in[:, 2 * n + 1, :], 1.0, 0.0,
                                         ALU.mult, ALU.add, lam_s[:, n:n + 1]).then_inc(lam_summed, 1)
            vec.wait_ge(ff_summed, 1)
            vec.wait_ge(dil_mask_made, 1)
            vec.tensor_scalar(fg[:, 0, :], ps[0:FOX, 4, :], bf_col[:, :], None, ALU.add).then_inc(gate_chain, 1)
            vec.wait_ge(gate_chain, 3)
            vec.scalar_tensor_tensor(fg[:, 1, :], fg[:, 0, :], -1.0, fg[:, 0, :], ALU.mult, ALU.max)\
               .then_inc(gate_chain, 1)
            vec.wait_ge(gate_exp, 2)
            vec.scalar_tensor_tensor(fg[:, 3, :], fg[:, 0, :], 0.0, fg[:, 1, :], ALU.min, ALU.subtract)\
               .then_inc(gate_chain, 1)
            vec.wait_ge(gate_chain, 5)
            vec.tensor_tensor_scan(fg[:, 2, :], fg[:, 3, :], fg[:, 3, :], 0.0, ALU.add, ALU.bypass)\
               .then_inc(gate_chain, 1)
            vec.wait_ge(lam_exp, 1)
            chain(vec.tensor_tensor(lam_s[:, 4:5], lam_s[:, 3:4], lam_s[:, 2:3], ALU.subtract))
            chain(vec.tensor_scalar(lam_s[:, 5:6], lam_s[:, 4:5], -LAM_INIT, None, ALU.add))
            chain(vec.tensor_scalar(diff_gain[:, :], diff_gain[:, :], 1.0 - LAM_INIT, None, ALU.mult))
            vec.memset(eps[:, :], LN_EPS).then_inc(eps_set, 1)
            vec.wait_ge(forget_turned, 1)
            vec.tensor_copy(forget_q[:, :, :], ps[:, 5, 0:TT * FOX].rearrange("p (i h) -> p i h", i=TT))\
               .then_inc(forget_q_ready, 1)
            for n in range(2 * MT):
                t, g = n // 2, n % 2
                vec.wait_ge(mem_hi_done, n + 1)
                sub_hi(mem_lo[:, 4 * g:4 * g + 4, t * P:(t + 1) * P],
                       ps[:, 4 + n, :].rearrange("p (k t) -> p k t", k=4),
                       mem_hi[:, 4 * g:4 * g + 4, t * P:(t + 1) * P]).then_inc(mem_lo_done, 1)

            def score(s):
                hp, i = STEPS[s]
                n = bias_item(s)
                w = (i + 1) * P
                lo = 0 if is_fox(hp) else SEQ - w
                vec.wait_ge(bias_made, n + 1)
                for m in maps_of(s):
                    vec.wait_ge(qk_done, m + 1)
                    c, before = prob_place(m)
                    if before < 0:
                        vec.wait_ge(forget_spread, FOX)
                    else:
                        vec.wait_ge(turned, before + 1)
                    vec.tensor_tensor_reduce(prob[:, c:c + w], ps[:, S_BANKS[m % len(S_BANKS)], 0:w],
                                             side[:, n % 4, lo:lo + w], -1.0, BIG, ALU.add, ALU.min,
                                             neg_max[:, m:m + 1]).then_inc(scored, 1)

            def mix(s):
                hp, i = STEPS[s]
                m0, m1 = maps_of(s)
                w = (i + 1) * P
                vec.wait_ge(exp_done, m1 + 1)
                chain(vec.reciprocal(mix_s[:, 0, s:s + 1], den[:, 1, s:s + 1]))
                chain(vec.scalar_tensor_tensor(mix_s[:, 1, s:s + 1], den[:, 0, s:s + 1], mix_s[:, 0, s:s + 1],
                                               lam_s[:, 5:6], ALU.mult, ALU.mult))
                c0, c1 = prob_place(m0)[0], prob_place(m1)[0]
                vec.scalar_tensor_tensor(prob[:, c0:c0 + w], prob[:, c1:c1 + w], mix_s[:, 1, s:s + 1],
                                         prob[:, c0:c0 + w], ALU.mult, ALU.add).then_inc(mixed, 1)

            def norm(s):
                hp, i = STEPS[s]
                c, _ = prob_place(maps_of(s)[0])
                row = prob[:, c:c + (i + 1) * P]
                vec.wait_ge(mixed, s + 1) if is_diff(hp) else vec.wait_ge(exp_done, maps_of(s)[0] + 1)
                chain(vec.reciprocal(den[:, 0, s:s + 1], den[:, 0, s:s + 1]))
                vec.tensor_scalar(row, row, den[:, 0, s:s + 1], None, ALU.mult).then_inc(normed, 1)

            def scale_pair(p):
                vec.wait_ge(rms_scaled, 2 * p + 2)
                vec.scalar_tensor_tensor(rms_t(p), ps[:, O_BANKS[p % 2], :], diff_gain[:, :], rms_t(p),
                                         ALU.mult, ALU.mult).then_inc(o_rmsed, 1)

            def output_low(p):
                src = rms_t(p) if is_diff(2 * p) else ps[:, O_BANKS[p % 2], :]
                kt = HEAD_ORDER[2 * p] // 2
                vec.wait_ge(o_hi_done, p + 1)
                sub_hi(act_lo[:, kt, :], src, act_hi[:, kt, :]).then_inc(o_lo_done, 1)

            for s in range(AHEAD):
                score(s)
            for k in range(N_STEPS + 1):
                if k + AHEAD < N_STEPS:
                    score(k + AHEAD)
                if k < N_STEPS:
                    if is_diff(STEPS[k][0]):
                        mix(k)
                    norm(k)
                if k % 8 == (PAIR_LAG + 1) % 8 and (k - PAIR_LAG) // 8 in TURN_OF_PAIR:
                    scale_pair((k - PAIR_LAG) // 8)
                if k % 8 == (PAIR_LAG + 2) % 8 and (k - PAIR_LAG) // 8 in TURN_OF_PAIR:
                    output_low((k - PAIR_LAG) // 8)
                if k % 8 == 1 and k >= 9 and not is_diff(2 * ((k - 1) // 8 - 1)):
                    output_low((k - 1) // 8 - 1)
            output_low(HEADS // 2 - 1)

            def add_residual(n, phase, units, h, t, bank=0):
                x_half = x_tok[:, t, HALF * h:HALF * (h + 1)]
                vec.wait_ge(dense_done, chunks_through(phase, units * h + units - 1) + t + 1)
                vec.scalar_tensor_tensor(x_half, x_half, ALPHA, ps[:, bank + t, :], ALU.mult, ALU.add).then_inc(res_done[n], 1)
                credits = TT if n < 2 else 0
                vec.wait_ge(res_done[n], credits + TT * h + t + 1)
                chain(vec.bn_stats(stats[:, t, h, :], x_half))

            def find_var(n, t):
                vec.bn_aggr(mean_var[:, t, :], stats[:, t, :, :].rearrange("p a b -> p (a b)")).then_inc(var_ready[n], 1)

            def layer_norm(n, phase):
                for t in range(TT):
                    add_residual(n, phase, 2, 0, t)

                def normalise(t):
                    vec.wait_ge(rstd_ready[n], t + 1)
                    vec.tensor_scalar(x_tok[:, t, :], x_tok[:, t, :], mean_var[:, t, 0:1], rstd[:, t:t + 1],
                                      ALU.subtract, ALU.mult).then_inc(z_ready[n], 1)

                for t in range(TT):
                    add_residual(n, phase, 2, 1, t)
                    find_var(n, t)
                    if t >= 1:
                        normalise(t - 1)
                normalise(TT - 1)
                if n == 0:
                    for k in range(2):
                        split_part(2 + k, chunks_through("mk", 1 + k))
                def apply(k):
                    vec.wait_ge(z_turned[n], k + 1)
                    if k >= 4:
                        vec.wait_ge(z_lo_done[n], k - 3)
                    vec.tensor_scalar(scratch[:, k % 4, :], ps[:, 4 + k % 4, :], ln_cols[:, 2 * n, k:k + 1],
                                      ln_cols[:, 2 * n + 1, k:k + 1], ALU.mult, ALU.add).then_inc(y_by_vec[n], 1)

                apply(1)
                for k in range(KT):
                    if k % 2 == 0 and 2 <= k:
                        apply(k + 1)
                    vec.wait_ge(z_hi_done[n], k + 1)
                    sub_hi(act_lo[:, k, :], scratch[:, k % 4, :], act_hi[:, k, :]).then_inc(z_lo_done[n], 1)
                vec.wait_ge(gains_loaded[n], 32)
                for t in range(TT):
                    chain(vec.tensor_tensor(x_tok[:, t, :], x_tok[:, t, :], side_gain[:, 0, :], ALU.mult))
                    vec.tensor_tensor(x_tok[:, t, :], x_tok[:, t, :], side_gain[:, 1, :], ALU.add)\
                       .then_inc(ln_applied[n], 1)

            layer_norm(0, "wo")

            for n in range(4):
                vec.wait_ge(mk_ready, n + 1)
                sub_hi(mem_kt_lo[:, 2 * n:2 * n + 2, :], ps[:, 4 + n, :].rearrange("p (f m) -> p f m", f=2),
                       mem_kt_hi[:, 2 * n:2 * n + 2, :]).then_inc(mk_split, 1)
            vec.wait_ge(mem_v_rounded, 1)
            sub_hi(mem_v_lo, mem_v[:, :, :], mem_v_hi).then_inc(mem_v_split, 1)
            for n in range(KT):
                vec.wait_ge(xq_hi_done, n + 1)
                vec.scalar_tensor_tensor(xq_lo[:, n, :], ps[:, n % 4, :], X_SCALE, xq_hi[:, n, :].bitcast(F32),
                                         ALU.mult, ALU.subtract).then_inc(mq_evac, 1)
            N_X = MEM_HEADS * TT

            def x_low(pair):
                h, i = pair // 2, 2 * (pair % 2)
                vec.wait_ge(xp_t_ready, pair + 1)
                for t in range(2):
                    cols = slice((i + t) * P, (i + t + 1) * P)
                    ins = sub_hi(xp_t_lo[:, h % 2, :, cols], ps[:, 6 + pair % 2, t * MT * P:(t + 1) * MT * P]
                                 .rearrange("p (m q) -> p m q", m=MT), xp_t_hi[:, h % 2, :, cols])
                ins.then_inc(xp_t_split, 1)

            def x_max(c):
                vec.wait_ge(xs_done, c + 1)
                vec.tensor_reduce(x_neg_max[:, c:c + 1], ps[:, X_S_BANKS[c % 4], 0:MEM], AX.X, ALU.max,
                                  negate=True).then_inc(x_maxed, 1)

            def x_scale(c):
                vec.wait_ge(x_exp_done, c + 1)
                chain(vec.reciprocal(x_rden[:, c:c + 1], x_den[:, c:c + 1]))
                vec.tensor_scalar(xp[:, c % 4, :], xp[:, c % 4, :], x_rden[:, c:c + 1], None, ALU.mult)\
                   .then_inc(x_scaled, 1)

            for c in range(X_AHEAD):
                x_max(c)
            for c in range(N_X + X_O_LAG + 1):
                if c + X_AHEAD < N_X:
                    x_max(c + X_AHEAD)
                if c < N_X:
                    x_scale(c)
                if c % 2 == 0 and 2 <= c <= N_X:
                    x_low(c // 2 - 1)
                if c >= TT + X_O_LAG and (c - TT - X_O_LAG) % TT == 0:
                    h = (c - TT - X_O_LAG) // TT
                    for f in range(2):
                        vec.wait_ge(xo_hi_done, 2 * h + f + 1)
                        sub_hi(act_lo[:, 2 * h + f, :], ps[:, X_O_BANK[h] + f, :], act_hi[:, 2 * h + f, :])\
                           .then_inc(xo_lo_done, 1)
            layer_norm(1, "mo")
            vec.wait_ge(ln_applied[1], TT)

            vec.sem_inc(gate_lo_done, 2)
            with vec.Fori(0, FT // 2) as t:
                def older_taps(q, tile0):
                    vec.wait_ge(tap2_done, 4 * t + (q + 1))
                    vec.scalar_tensor_tensor(scratch[:, q, 1:SEQ], ps[:, q, 0:SEQ - 1],
                                             conv_cols[:, 1, bass.ds(2 * t + tile0, 1)], scratch[:, q, 1:SEQ],
                                             ALU.mult, ALU.add).then_inc(tap1_done, 1)
                    vec.wait_ge(tap1_done, 4 * t + (q + 1))
                    vec.scalar_tensor_tensor(scratch[:, q, 2:SEQ], ps[:, q, 0:SEQ - 2],
                                             conv_cols[:, 0, bass.ds(2 * t + tile0, 1)], scratch[:, q, 2:SEQ],
                                             ALU.mult, ALU.add).then_inc(conv_done, 1)

                for q, tile0 in enumerate([0, 1, FT, FT + 1]):
                    older_taps(q, tile0)
                for q in range(2):
                    vec.wait_ge(gelu_done, 2 * t + (2 + q + 1))
                    vec.wait_ge(conv_done, 4 * t + (4 + q + 3))
                    vec.wait_ge(gate_lo_done, 2 * t + (q + 1))
                    vec.tensor_tensor(side[:, 2 + q, :], side[:, q, :], scratch[:, 2 + q, :], ALU.mult)\
                       .then_inc(gated, 1)
                for q in range(2):
                    vec.wait_ge(gate_hi_done, 2 * t + (q + 1))
                    tile = bass.ds(2 * t + q, 1)
                    vec.tensor_tensor(gate_lo[:, tile, :].rearrange("p a b -> p (a b)"), side[:, 2 + q, :],
                                      gate_hi[:, tile, :].rearrange("p a b -> p (a b)").bitcast(F32),
                                      ALU.subtract).then_inc(gate_lo_done, 1)

            for t in range(TT):
                add_residual(2, "down", 6, 0, t, 4)
            vec.wait_ge(gains_loaded[2], 32)

            for t in range(TT):
                add_residual(2, "down", 6, 1, t)
                find_var(2, t)
                vec.wait_ge(var_ready[2], t + 1)
                if t < TT - 1:
                    vec.tensor_scalar(neg_mean[:, t:t + 1], mean_var[:, t, 0:1], -1.0, None, ALU.mult)\
                       .then_inc(neg_mean_ready, 1)
            third = x_tok[:, 2, :]
            vec.wait_ge(last_z_ready, 3)
            vec.tensor_tensor(third, third, side_gain[:, 0, :], ALU.mult).then_inc(third_gained, 1)
            last = x_tok[:, TT - 1, :]
            for h in range(2):
                cols = slice(HALF * h, HALF * (h + 1))
                vec.scalar_tensor_tensor(last[:, cols], last[:, cols], mean_var[:, TT - 1, 0:1],
                                         side_gain[:, 0, cols], ALU.subtract, ALU.mult).then_inc(last_half_gained, 1)
            vec.wait_ge(rstd_ready[2], 1)
            for h in range(2):
                cols = slice(HALF * h, HALF * (h + 1))
                vec.wait_ge(last_half_gained, h + 1)
                vec.scalar_tensor_tensor(last[:, cols], last[:, cols], rstd[:, TT - 1:TT], side_gain[:, 1, cols],
                                         ALU.mult, ALU.add).then_inc(last_half_done, 1)
            vec.wait_ge(third_gained, 1)
            vec.tensor_tensor(third, third, side_gain[:, 1, :], ALU.add).then_inc(third_done, 1)


_INS = ["x", "mem", "w_in", "b_f", "lambda_q1", "lambda_k1", "lambda_q2", "lambda_k2", "diff_norm_g", "w_o",
        "ln1_g", "ln1_b", "w_mq", "w_mkv", "w_mo", "ln2_g", "ln2_b", "w_up", "conv_w", "conv_b", "w_down",
        "ln3_g", "ln3_b"]
_OUTS = [((1, SEQ, D), "float32")]


def kernel(**inputs):
    import numpy as _np
    import concourse.bacc as _bacc
    from concourse import mybir as _mybir
    from concourse.bass_utils import run_bass_kernel_spmd as _run

    nc = _bacc.Bacc("TRN2", target_bir_lowering=False, num_devices=1)
    arrays, args = {}, []
    for name in _INS:
        a = _np.ascontiguousarray(inputs[name])
        arrays[f"in_{name}_dram"] = a
        args.append(nc.dram_tensor(f"in_{name}_dram", a.shape, _mybir.dt.from_np(a.dtype), kind="ExternalInput").ap())
    for i, (shape, dtype) in enumerate(_OUTS):
        dt = _mybir.dt.from_np(_np.dtype(dtype))
        args.append(nc.dram_tensor(f"out_{i}_dram", shape, dt, kind="ExternalOutput").ap())
    build_layer(nc, *args)
    r = _run(nc, [arrays], core_ids=[0])
    return r.results[0]["out_0_dram"]
```
